# Optimizing a Trainium2 kernel written in Bass

```python
import math
import numpy as np
import jax
import jax.numpy as jnp
from jax import lax

D_MODEL = 1024
BATCH = 1
SEQ = 1024
DEPTH = 2

HEAD_DIM = 64
NSA_HEADS = 4
NSA_KV_HEADS = 1
CMP_BLOCK = 32
CMP_STRIDE = 16
SEL_BLOCK = 64
SEL_TOPK = 16
NSA_WINDOW = 512
DIL_PATTERNS = ((128, 1), (512, 4), (2048, 16))
DIL_HEADS_PER_GROUP = 2
DIL_HEADS = DIL_HEADS_PER_GROUP * len(DIL_PATTERNS)
SWA_HEADS = 6
SWA_KV_HEADS = 2
SWA_WINDOW = 128
BLOCK_Q = 128
D_FF = 2816
CONV_WIDTH = 3
ROPE_THETA = 10000.0
RMS_EPS = 1e-6
NEG = -1e30
TINY = 1e-30
FORCE = 1e4
COL_SIZES = ((NSA_HEADS * HEAD_DIM,) + (NSA_KV_HEADS * HEAD_DIM,) * 6 + (3 * NSA_HEADS,)
             + (DIL_HEADS * HEAD_DIM,) * 3
             + (SWA_HEADS * HEAD_DIM, SWA_KV_HEADS * HEAD_DIM, SWA_KV_HEADS * HEAD_DIM))
IN_COLS = sum(COL_SIZES)
MIX_WIDTH = (NSA_HEADS + DIL_HEADS + SWA_HEADS) * HEAD_DIM

kernel_name = 'hybrid_nsa_dilated_swa_convffn_trunk'

def _rmsnorm(x, w):
    xf = x.astype(jnp.float32)
    y = xf * lax.rsqrt(jnp.mean(xf * xf, axis=-1, keepdims=True) + RMS_EPS)
    return (y * w.astype(jnp.float32)).astype(x.dtype)

def _rope_tables(positions, dtype):
    inv = ROPE_THETA ** (-jnp.arange(0, HEAD_DIM, 2, dtype=jnp.float32) / HEAD_DIM)
    ang = positions.astype(jnp.float32)[..., None] * inv
    return (jnp.cos(ang)[:, :, None, :].astype(dtype),
            jnp.sin(ang)[:, :, None, :].astype(dtype))

def _apply_rope(t, cos, sin):
    t1, t2 = jnp.split(t, 2, axis=-1)
    return jnp.concatenate([t1 * cos - t2 * sin, t2 * cos + t1 * sin], axis=-1)

def _masked_softmax(s, mask):
    s = jnp.where(mask, s, NEG)
    m = jnp.max(s, axis=-1, keepdims=True)
    p = jnp.where(mask, jnp.exp(s - m), 0.0)
    return p / jnp.maximum(jnp.sum(p, axis=-1, keepdims=True), TINY)

def _band_blocks(t, n_prev, block):
    B, S = t.shape[:2]
    nb = S // block
    tb = t.reshape((B, nb, block) + t.shape[2:])
    tp = jnp.pad(tb, [(0, 0), (n_prev, 0)] + [(0, 0)] * (tb.ndim - 2))
    return jnp.concatenate([tp[:, i:i + nb] for i in range(n_prev + 1)], axis=2)

def _banded_attention(q, k, v, max_dist, block, sinks=None, return_lse=False):
    B, S, Hk, G, hd = q.shape
    block = math.gcd(block, S)
    nb = S // block
    n_prev = -(-max_dist // block)
    span = (n_prev + 1) * block
    kw = _band_blocks(k, n_prev, block)
    vw = _band_blocks(v, n_prev, block)
    qb = q.reshape(B, nb, block, Hk, G, hd)
    s = jnp.einsum('bnqhgd,bnkhd->bnhgqk', qb, kw).astype(jnp.float32) * (hd ** -0.5)
    dist = jnp.arange(block)[:, None] + n_prev * block - jnp.arange(span)[None, :]
    kpos = jnp.arange(nb)[:, None] * block - n_prev * block + jnp.arange(span)[None, :]
    mask = ((dist >= 0) & (dist <= max_dist))[None] & (kpos >= 0)[:, None, :]
    mask = mask[None, :, None, None]
    s = jnp.where(mask, s, NEG)
    m = jnp.max(s, axis=-1, keepdims=True)
    if sinks is not None:
        sk = sinks.astype(jnp.float32).reshape(1, 1, Hk, G, 1, 1)
        m = jnp.maximum(m, sk)
    p = jnp.where(mask, jnp.exp(s - m), 0.0)
    l = jnp.sum(p, axis=-1, keepdims=True)
    if sinks is not None:
        l = l + jnp.exp(sk - m)
    o = jnp.einsum('bnhgqk,bnkhd->bnqhgd', (p / l).astype(v.dtype), vw).reshape(B, S, Hk, G, hd)
    if not return_lse:
        return o
    lse = (m + jnp.log(l))[..., 0].transpose(0, 1, 4, 2, 3).reshape(B, S, Hk, G)
    return o, lse

def _compress(t, w, pe):
    B, S, Hk, hd = t.shape
    r = CMP_BLOCK // CMP_STRIDE
    n = S // CMP_STRIDE
    ts = t.reshape(B, n, CMP_STRIDE, Hk, hd)
    blocks = jnp.concatenate([ts[:, i:n - r + 1 + i] for i in range(r)], axis=2)
    return jnp.einsum('bnlhd,lde->bnhe', blocks + pe[:, None, :], w)

def _nsa(q, k_c, v_c, k_s, v_s, k_w, v_w, gates, w_ck, w_cv, pe_k, pe_v):
    B, S, Hk, G, hd = q.shape
    kc = _compress(k_c, w_ck, pe_k)
    vc = _compress(v_c, w_cv, pe_v)
    n_cmp = kc.shape[1]
    n_sel = S // SEL_BLOCK
    top = min(SEL_TOPK, n_sel)
    cmp_end = jnp.arange(n_cmp) * CMP_STRIDE + CMP_BLOCK - 1
    ci = jnp.arange(n_cmp)[:, None] * CMP_STRIDE
    sj = jnp.arange(n_sel)[None, :] * SEL_BLOCK
    overlap = ((ci < sj + SEL_BLOCK) & (ci + CMP_BLOCK > sj)).astype(jnp.float32)
    ks_blk = k_s.reshape(B, n_sel, SEL_BLOCK, Hk, hd).transpose(0, 3, 1, 2, 4)
    vs_blk = v_s.reshape(B, n_sel, SEL_BLOCK, Hk, hd).transpose(0, 3, 1, 2, 4)
    nb = S // BLOCK_Q
    q_blocks = q.reshape(B, nb, BLOCK_Q, Hk, G, hd).transpose(1, 0, 2, 3, 4, 5)
    scale = hd ** -0.5
    gather = jax.vmap(jax.vmap(lambda blk, ids: blk[ids]))

    def per_block(args):
        qb, b = args
        t = b * BLOCK_Q + jnp.arange(BLOCK_Q)
        s = jnp.einsum('bqhgd,bnhd->bhgqn', qb, kc).astype(jnp.float32) * scale
        p = _masked_softmax(s, cmp_end[None, :] <= t[:, None])
        o_cmp = jnp.einsum('bhgqn,bnhd->bqhgd', p.astype(vc.dtype), vc)
        imp = jnp.einsum('bhgqn,nj->bhqj', p, overlap)
        blk = jnp.arange(n_sel)[None, :]
        cur = (t // SEL_BLOCK)[:, None]
        forced = (blk == 0) | (blk == cur) | (blk == cur - 1)
        imp = jnp.where(forced, FORCE, imp)
        imp = jnp.where(blk <= cur, imp, NEG)
        val, idx = lax.top_k(imp, top)
        ks = gather(ks_blk, idx)
        vs = gather(vs_blk, idx)
        s2 = jnp.einsum('bqhgd,bhqkld->bhgqkl', qb, ks).astype(jnp.float32) * scale
        kpos = idx[..., None] * SEL_BLOCK + jnp.arange(SEL_BLOCK)
        m2 = (val[..., None] > NEG / 2) & (kpos <= t[:, None, None])
        n_k = top * SEL_BLOCK
        p2 = _masked_softmax(s2.reshape(B, Hk, G, BLOCK_Q, n_k), m2.reshape(B, Hk, 1, BLOCK_Q, n_k))
        o_sel = jnp.einsum('bhgqn,bhqnd->bqhgd', p2.astype(vs.dtype), vs.reshape(B, Hk, BLOCK_Q, n_k, hd))
        return o_cmp, o_sel

    o_cmp, o_sel = lax.map(per_block, (q_blocks, jnp.arange(nb)))
    o_cmp = o_cmp.transpose(1, 0, 2, 3, 4, 5).reshape(B, S, Hk, G, hd)
    o_sel = o_sel.transpose(1, 0, 2, 3, 4, 5).reshape(B, S, Hk, G, hd)
    o_win = _banded_attention(q, k_w, v_w, NSA_WINDOW - 1, BLOCK_Q)
    return gates[..., 0:1] * o_cmp + gates[..., 1:2] * o_sel + gates[..., 2:3] * o_win

def _dilated_group(q, k, v, window, dilation):
    B, S, H, hd = q.shape
    n = S // dilation

    def fold(t):
        return t.reshape(B, n, dilation, H, hd).transpose(0, 2, 1, 3, 4).reshape(B * dilation, n, H, hd)

    o, lse = _banded_attention(fold(q)[:, :, :, None], fold(k), fold(v), window // dilation, BLOCK_Q,
                               return_lse=True)
    o = o[:, :, :, 0].reshape(B, dilation, n, H, hd).transpose(0, 2, 1, 3, 4).reshape(B, S, H, hd)
    lse = lse[..., 0].reshape(B, dilation, n, H).transpose(0, 2, 1, 3).reshape(B, S, H)
    return o, lse

def _token_mixers(h, cos, sin, w_in, w_out, w_ck, w_cv, pe_k, pe_v, sinks):
    B, S, _ = h.shape
    proj = h @ w_in
    split_at = np.cumsum(COL_SIZES)[:-1].tolist()
    (a_q, a_kc, a_vc, a_ks, a_vs, a_kw, a_vw, a_g,
     b_q, b_k, b_v, c_q, c_k, c_v) = jnp.split(proj, split_at, axis=-1)

    def heads(t, n):
        return t.reshape(B, S, n, HEAD_DIM)

    def rope(t):
        return _apply_rope(t, cos, sin)

    ga = NSA_HEADS // NSA_KV_HEADS
    qa = rope(heads(a_q, NSA_HEADS)).reshape(B, S, NSA_KV_HEADS, ga, HEAD_DIM)
    gates = jax.nn.sigmoid(a_g).reshape(B, S, NSA_KV_HEADS, ga, 3)
    out_a = _nsa(qa,
                 rope(heads(a_kc, NSA_KV_HEADS)), heads(a_vc, NSA_KV_HEADS),
                 rope(heads(a_ks, NSA_KV_HEADS)), heads(a_vs, NSA_KV_HEADS),
                 rope(heads(a_kw, NSA_KV_HEADS)), heads(a_vw, NSA_KV_HEADS),
                 gates, w_ck, w_cv, pe_k, pe_v).reshape(B, S, NSA_HEADS * HEAD_DIM)

    qb, kb, vb = rope(heads(b_q, DIL_HEADS)), rope(heads(b_k, DIL_HEADS)), heads(b_v, DIL_HEADS)
    outs, lses = [], []
    for g, (win, dil) in enumerate(DIL_PATTERNS):
        sl = slice(g * DIL_HEADS_PER_GROUP, (g + 1) * DIL_HEADS_PER_GROUP)
        o, lse = _dilated_group(qb[:, :, sl], kb[:, :, sl], vb[:, :, sl], win, dil)
        outs.append(o)
        lses.append(lse)
    alpha = jax.nn.softmax(jnp.stack(lses, axis=0), axis=0)
    out_b = jnp.concatenate([o * alpha[g][..., None].astype(o.dtype) for g, o in enumerate(outs)],
                            axis=2).reshape(B, S, DIL_HEADS * HEAD_DIM)

    gc = SWA_HEADS // SWA_KV_HEADS
    qc = rope(heads(c_q, SWA_HEADS)).reshape(B, S, SWA_KV_HEADS, gc, HEAD_DIM)
    out_c = _banded_attention(qc, rope(heads(c_k, SWA_KV_HEADS)), heads(c_v, SWA_KV_HEADS),
                              SWA_WINDOW - 1, BLOCK_Q,
                              sinks=sinks.reshape(SWA_KV_HEADS, gc)).reshape(B, S, SWA_HEADS * HEAD_DIM)

    return jnp.concatenate([out_a, out_b, out_c], axis=-1) @ w_out

def _conv_ffn(h, w_gate, w_up, conv_w, conv_b, w_down):
    S = h.shape[1]
    g = h @ w_gate
    gp = jnp.pad(g, ((0, 0), (CONV_WIDTH - 1, 0), (0, 0)))
    acc = gp[:, 0:S] * conv_w[0]
    for i in range(1, CONV_WIDTH):
        acc = acc + gp[:, i:i + S] * conv_w[i]
    return (jax.nn.gelu(acc + conv_b, approximate=True) * (h @ w_up)) @ w_down

def setup_inputs(seed: int = 0) -> dict:
    key = jax.random.key(seed)
    ks = jax.random.split(key, 20)
    f32 = jnp.float32

    def nrm(k, shape, scale):
        return jax.random.normal(k, shape, f32) * scale

    x = nrm(ks[0], (BATCH, SEQ, D_MODEL), 1.0)
    c = nrm(ks[1], (BATCH, D_MODEL), 1.0)
    offset = jax.random.randint(ks[2], (BATCH, 1), 0, 4096, dtype=jnp.int32)
    positions = jnp.arange(SEQ, dtype=jnp.int32)[None, :] + offset
    w_in = nrm(ks[3], (DEPTH, D_MODEL, IN_COLS), D_MODEL ** -0.5)
    w_out = nrm(ks[4], (DEPTH, MIX_WIDTH, D_MODEL), MIX_WIDTH ** -0.5)
    w_ada = nrm(ks[5], (DEPTH, D_MODEL, 6 * D_MODEL), 0.5 * D_MODEL ** -0.5)
    b_ada = nrm(ks[6], (DEPTH, 6 * D_MODEL), 0.01)
    norm_w = 1.0 + nrm(ks[7], (DEPTH, 4, D_MODEL), 0.05)
    cmp_w_k = nrm(ks[8], (DEPTH, CMP_BLOCK, HEAD_DIM, HEAD_DIM), (CMP_BLOCK * HEAD_DIM) ** -0.5)
    cmp_w_v = nrm(ks[9], (DEPTH, CMP_BLOCK, HEAD_DIM, HEAD_DIM), (CMP_BLOCK * HEAD_DIM) ** -0.5)
    cmp_pe_k = nrm(ks[10], (DEPTH, CMP_BLOCK, HEAD_DIM), 0.5)
    cmp_pe_v = nrm(ks[11], (DEPTH, CMP_BLOCK, HEAD_DIM), 0.5)
    sinks = nrm(ks[12], (DEPTH, SWA_HEADS), 1.0)
    w_gate = nrm(ks[13], (DEPTH, D_MODEL, D_FF), D_MODEL ** -0.5)
    w_up = nrm(ks[14], (DEPTH, D_MODEL, D_FF), D_MODEL ** -0.5)
    conv_w = nrm(ks[15], (DEPTH, CONV_WIDTH, D_FF), CONV_WIDTH ** -0.5)
    conv_b = nrm(ks[16], (DEPTH, D_FF), 0.01)
    w_down = nrm(ks[17], (DEPTH, D_FF, D_MODEL), D_FF ** -0.5)
    return {'x': x, 'c': c, 'positions': positions, 'w_in': w_in, 'w_out': w_out,
            'w_ada': w_ada, 'b_ada': b_ada, 'norm_w': norm_w,
            'cmp_w_k': cmp_w_k, 'cmp_w_v': cmp_w_v, 'cmp_pe_k': cmp_pe_k, 'cmp_pe_v': cmp_pe_v,
            'sinks': sinks, 'w_gate': w_gate, 'w_up': w_up, 'conv_w': conv_w, 'conv_b': conv_b,
            'w_down': w_down}

def reference(x, c, positions, w_in, w_out, w_ada, b_ada, norm_w, cmp_w_k, cmp_w_v, cmp_pe_k, cmp_pe_v,
              sinks, w_gate, w_up, conv_w, conv_b, w_down):
    cos, sin = _rope_tables(positions, x.dtype)
    cond = jax.nn.silu(c)
    for layer in range(DEPTH):
        ada = cond @ w_ada[layer] + b_ada[layer]
        sh1, sc1, g1, sh2, sc2, g2 = [a[:, None, :] for a in jnp.split(ada, 6, axis=-1)]
        h = _rmsnorm(x, norm_w[layer, 0]) * (1 + sc1) + sh1
        h = _token_mixers(h, cos, sin, w_in[layer], w_out[layer], cmp_w_k[layer], cmp_w_v[layer],
                          cmp_pe_k[layer], cmp_pe_v[layer], sinks[layer])
        x = x + g1 * _rmsnorm(h, norm_w[layer, 1])
        h = _rmsnorm(x, norm_w[layer, 2]) * (1 + sc2) + sh2
        h = _conv_ffn(h, w_gate[layer], w_up[layer], conv_w[layer], conv_b[layer], w_down[layer])
        x = x + g2 * _rmsnorm(h, norm_w[layer, 3])
    return x


_drawn_inputs = setup_inputs


def setup_inputs(seed=0):
    import zlib

    import numpy as np

    out = dict(_drawn_inputs(seed))
    spreads = {}
    factors = {'cmp_pe_k': 8.0, 'sinks': 8.0, 'conv_b': 8.0}
    for name, (base, spread) in spreads.items():
        noise = np.random.default_rng([zlib.crc32(name.encode()), seed]).standard_normal(out[name].shape)
        drawn = base * np.exp(spread * noise) if base else spread * noise
        out[name] = jnp.asarray(drawn.astype(out[name].dtype))
    for name, factor in factors.items():
        out[name] = (out[name] * factor).astype(out[name].dtype)
    return out
```

```python
from contextlib import ExitStack

import concourse.bass as bass
from concourse import mybir

F32 = mybir.dt.float32
F32R = mybir.dt.float32r
BF16 = mybir.dt.bfloat16
I32 = mybir.dt.int32
ALU = mybir.AluOpType
ACT = mybir.ActivationFunctionType
AX = mybir.AxisListType

P = 128
D = 1024
S = 1024
DEPTH = 2
HD = 64
FF = 2816
KT_D = D // P
NS = S // P
HALF = 512
NH = S // HALF
FT = FF // P
N_CMP = S // 16 - 1
CMP_L = 32
NEG = -1e30
FLOOR = -1e28
TINY = 1e-30
EPS = 1e-6
SCALE = HD ** -0.5
THETA = 10000.0
WIN_TILES = 512 // P
MROW = 64

A_Q, A_KC, A_VC, A_KS, A_VS, A_KW, A_VW, A_G = 0, 256, 320, 384, 448, 512, 576, 640
B_Q, B_K, B_V = 652, 1036, 1420
C_Q, C_K, C_V = 1804, 2188, 2316

STAGES = [
    dict(kind="A", passes=[[(A_Q, 320)], [(A_VC, 332)]]),
    dict(kind="C", kv=0, passes=[[(C_Q, 192), (C_K, 64), (C_V, 64)]]),
    dict(kind="C", kv=1, passes=[[(C_Q + 192, 192), (C_K + 64, 64), (C_V + 64, 64)]]),
    dict(kind="B", kv=0, passes=[[(B_Q, 128), (B_K, 128), (B_V, 128)]]),
    dict(kind="B", kv=1, passes=[[(B_Q + 128, 128), (B_K + 128, 128), (B_V + 128, 128)]]),
    dict(kind="B", kv=2, passes=[[(B_Q + 256, 128), (B_K + 256, 128), (B_V + 256, 128)]]),
]
LAYOUTS = {
    "A0": dict(rope=(0, 5, 64), jobs=[(0, "Q", 0), (64, "Q", 1), (128, "Q", 2), (192, "Q", 3), (256, "KC", 0)],
               values=[]),
    "A1": dict(rope=(64, 2, 128), jobs=[(0, "VC", 0), (64, "K", 0), (192, "K", 1)],
               values=[(128, 0), (256, 1)]),
    "C": dict(rope=(0, 4, 64), jobs=[(0, "Q", 0), (64, "Q", 1), (128, "Q", 2), (192, "K", 0)], values=[(256, 0)]),
    "B": dict(rope=(0, 4, 64), jobs=[(0, "Q", 2), (64, "Q", 3), (128, "K", 0), (192, "K", 1)],
              values=[(256, 0), (320, 1)]),
}
BQ = 2


POOL_STEPS, ACT_STEPS, DVE_STEPS = 226, 101, 570

def spread(n, most):
    k = -(-n // most)
    return [n // k + (i < n % k) for i in range(k)]


def chunk_list(tiles, masks, lhs, kv):
    out, at = [], 0
    for n in spread(len(tiles), 4):
        ts = tiles[at:at + n]
        at += n
        out.append(dict(lhs=lhs, kv=kv, key0=ts[0] * P, cols=n * P,
                        masks=[(masks[t], (t - ts[0]) * P) for t in ts if t in masks]))
    return out


def tasks_of(stage):
    kind = stage["kind"]
    out = []
    if kind == "A":
        for i in range(NS):
            cols = []
            win = list(range(max(0, i - WIN_TILES), i + 1))
            for br in range(3):
                for h in range(4):
                    lhs = (h, i * P)
                    if br == 0:
                        cols.append([dict(lhs=lhs, kv="cmp", key0=0, cols=P, masks=[(("cmpS", i), 0)])])
                    elif br == 1:
                        cols.append(chunk_list(list(range(i + 1)), {i: "C"}, lhs, 0))
                    else:
                        m = {i: "C"}
                        if i >= WIN_TILES:
                            m[i - WIN_TILES] = "E"
                        cols.append(chunk_list(win, m, lhs, 1))
            grp = lambda: [dict(q=(0, 4), q0=i * P, n=P, out=0)]
            subs = [dict(br=0, units=[dict(kv="cmp", key=0, groups=grp(), mask=("cmpT", i))]),
                    dict(br=1, units=[dict(kv=0, key=t, groups=grp(), mask="CT" if t == i else None)
                                      for t in range(i + 1)]),
                    dict(br=2, units=[dict(kv=1, key=t, groups=grp(),
                                           mask="CT" if t == i else ("ET" if t == i - WIN_TILES else None))
                                      for t in win])]
            out.append(dict(i=i, lanes=4, cols=cols, subs=subs, rows=12))
    elif kind == "C":
        for i in range(NS):
            ts = list(range(max(0, i - 1), i + 1))
            m = {i: "C", i - 1: "E"}
            cols = [chunk_list(ts, m, (h, i * P), 0) for h in range(3)]
            units = [dict(kv=0, key=t, groups=[dict(q=(0, 3), q0=i * P, n=P, out=0)],
                          mask="CT" if t == i else "ET") for t in ts]
            out.append(dict(i=i, lanes=3, cols=cols, subs=[dict(br=0, units=units)], rows=3))
    else:
        for g in range(NS // 2):
            cols = []
            for h in range(2):
                for b in range(2):
                    blk = 2 * g + b
                    if stage["kv"] == 2:
                        ts, m = [blk], {blk: "B"}
                    else:
                        first = max(0, blk - 1) if stage["kv"] == 0 else max(2 * g, blk - 1)
                        ts = list(range(first, blk + 1))
                        m = {blk: "C", blk - 1: "F"}
                    cols.append(chunk_list(ts, m, (BQ + h, blk * P), h))
            grp = lambda: [dict(q=(BQ + h, 1), q0=2 * g * P, n=2 * P, out=h * 2 * P, kv=h) for h in range(2)]
            if stage["kv"] == 2:
                units = [dict(key=2 * g, mask="BT|"), dict(key=2 * g + 1, mask="|BT")]
            else:
                units = [dict(key=2 * g, mask="CT|FT"), dict(key=2 * g + 1, mask="|CT")]
                if stage["kv"] == 0 and g > 0:
                    units = [dict(key=2 * g - 1, mask="FT|")] + units
            for u in units:
                u["kv"] = None
                u["groups"] = grp()
            out.append(dict(i=g, lanes=4, cols=cols, subs=[dict(br=0, units=units)], rows=4))
    return out


LAG = 2
EARLY = 2


def steps_of(stage, n):
    tasks = tasks_of(stage)
    for t in tasks:
        t["ord"] = n["task"]
        n["task"] += 1
        t["chunks"] = []
        for r, col in enumerate(t["cols"]):
            for j, c in enumerate(col):
                c.update(ord=n["chunk"], row=r, j=j)
                n["chunk"] += 1
                t["chunks"].append(c)
        for s in t["subs"]:
            s.update(ord=n["sub"], task=t)
            n["sub"] += 1
            for k, u in enumerate(s["units"]):
                u.update(ord=n["unit"], sub=s, first=k == 0, last=k == len(s["units"]) - 1, task=t)
                n["unit"] += 1
    units = [u for t in tasks for s in t["subs"] for u in s["units"]]
    at_unit = [[] for _ in units]
    steps, start = [], 0
    for t in tasks:
        first = units.index(t["subs"][0]["units"][0])
        end = first - EARLY
        if end <= 0:
            steps += [("S", c) for c in t["chunks"]] + [("M", t)]
        else:
            room = range(max(start, 0), end)
            many, k = spread(len(t["chunks"]), -(-len(t["chunks"]) // len(room))), 0
            many = [0] * (len(room) - len(many)) + many
            for x, m in zip(room, many):
                at_unit[x] += [("S", c) for c in t["chunks"][k:k + m]]
                k += m
            at_unit[end - 1].append(("M", t))
        start = end
        if first <= 1:
            steps.append(("MT", t))
        else:
            at_unit[first - 2].append(("MT", t))
    waiting_pv, waiting_t = [], []

    def pv(u):
        steps.append(("PV", u))
        for w in waiting_t:
            steps.append(("T", w))
        waiting_t.clear()
        if u["last"]:
            waiting_t.append(u["sub"])

    for u, more in zip(units, at_unit):
        steps.append(("ST", u))
        if waiting_pv:
            steps.append(("R", waiting_pv[-1]))
        steps += more
        waiting_pv.append(u)
        if len(waiting_pv) > LAG:
            pv(waiting_pv.pop(0))
    steps.append(("R", waiting_pv[-1]))
    for u in waiting_pv:
        pv(u)
    for w in waiting_t:
        steps.append(("T", w))
    return steps


class Plan:

    def __init__(self):
        n = dict(chunk=0, task=0, unit=0, sub=0)
        self.stages = []
        job = 0
        pn = 0
        for st in STAGES:
            s = dict(st)
            s["unit0"] = n["unit"]
            s["sub0"] = n["sub"]
            s["steps"] = steps_of(st, n)
            s["unit1"] = n["unit"]
            s["sub1"] = n["sub"]
            s["dists"] = []
            for k, cols in enumerate(st["passes"]):
                lay = LAYOUTS[st["kind"] + (str(k) if st["kind"] == "A" else "")]
                jobs = [dict(col=c, what=w, slot=sl, half=h, ord=job + 2 * x + h)
                        for x, (c, w, sl) in enumerate(lay["jobs"]) for h in range(NH)]
                job += len(jobs)
                s["dists"].append(dict(cols=cols, width=sum(c for _, c in cols), lay=lay, jobs=jobs, ord=pn))
                pn += 1
            self.stages.append(s)
        self.n, self.jobs, self.proj = n, job, pn
        self.tiles = []
        self.passes = []
        for s in self.stages:
            for d in s["dists"]:
                d["pass"] = self.add("in", [("w_in", k, d["cols"]) for k in range(KT_D)], d["width"])
        self.out_pass = [self.add("out", [("w_out", k, [(n * HALF, HALF)]) for k in range(KT_D)], HALF)
                         for n in range(NH)]
        self.gu, self.dn = {}, {}
        G = FT // 2
        self.gu[0] = self.add("gu", [("gu", k, 0) for k in range(KT_D)], HALF)
        for g in range(G):
            if g + 1 < G:
                self.gu[g + 1] = self.add("gu", [("gu", k, g + 1) for k in range(KT_D)], HALF)
            self.dn[g] = [self.add("dn", [("w_down", 2 * g + j, [(n * HALF, HALF)]) for j in range(2)], HALF)
                          for n in range(NH)]
        self.G = G

    def add(self, kind, tiles, width):
        p = dict(kind=kind, w0=len(self.tiles), n=len(tiles), width=width, ord=len(self.passes))
        self.tiles += [dict(spec=t, width=width, p=p) for t in tiles]
        self.passes.append(p)
        return p


def trunk(nc, x, c, positions, w_in, w_out, w_ada, b_ada, norm_w, cmp_w_k, cmp_w_v, cmp_pe_k, cmp_pe_v,
          sinks, w_gate, w_up, conv_w, conv_b, w_down, out):
    plan = Plan()
    G = plan.G
    mix_dram = nc.dram_tensor("mix_rows", (S, D), F32).ap()
    v_dram = nc.dram_tensor("value_rows", (S, P), F32).ap()
    out2 = out[0]
    x2 = x[0]

    with ExitStack() as ctx:
        def sb(name, shape, dt=F32, where=ctx):
            return where.enter_context(nc.sbuf_tensor(name, shape, dt))

        def sem(name):
            return ctx.enter_context(nc.semaphore(name))

        hT_hi = sb("hT_hi", [P, KT_D, S], F32R)
        hT_lo = sb("hT_lo", [P, KT_D, S], F32R)
        NRAW, NW = 4, 3
        w_raw = sb("w_raw", [P, NRAW, HALF])
        w_hi = sb("w_hi", [P, NW, HALF], F32R)
        w_lo = sb("w_lo", [P, NW, HALF], F32R)
        ident = sb("ident", [P, P])
        ident_b = sb("ident_b", [P, P], BF16)
        strip_T = sb("strip_T", [P, 4, P], BF16)
        strip_BT = sb("strip_BT", [P, 3, P], BF16)
        edge_T = sb("edge_T", [P, P], BF16)
        cmp_T = sb("cmp_T", [P, S], BF16)
        fc_S = sb("fc_S", [P, 2, P], BF16)
        e_S = sb("e_S", [P, P], BF16)
        b_S = sb("b_S", [P, P], BF16)
        CMP_OFF = 8 * (NS - 1)
        cmp_S = sb("cmp_S", [P, CMP_OFF + P], BF16)
        lane_mask = sb("lane_mask", [12, 4, P], BF16)
        row_ones = sb("row_ones", [12, 3])
        sel_m = sb("sel_m", [MROW + 4, 66], F32R)
        ones = sb("ones", [P, P])
        cos_t = sb("cos_t", [P, NS, 32])
        sin_t = sb("sin_t", [P, NS, 32])
        cond = sb("cond", [P, KT_D])
        nw_col = sb("nw_col", [P, 2, KT_D])
        aff_a = sb("aff_a", [P, 2, KT_D])
        aff_b = sb("aff_b", [P, 2, KT_D])
        stat = sb("stat", [P, 6, NS])
        gates = sb("gates", [P, NS, 12])
        sink_b = sb("sink_b", [P, 2, 6])
        pe_col = sb("pe_col", [P, CMP_L])
        cw = sb("cw", [P, 3, FT])
        cb = sb("cb", [P, FT])

        at = ExitStack()
        over_q = ExitStack()
        u_T0 = sb("u_T0", [66, 2, S], F32, over_q)
        sb("u_gap", [66, 2, S], F32, over_q)
        u_T1 = sb("u_T1", [66, 2, S], F32, over_q)
        over_q.close()
        q_hh = sb("q_hh", [P, 4, S], F32R, at)
        q_lm = sb("q_lm", [MROW + 12, 4, S], F32R, at)
        k_hl = sb("k_hl", [P, 2, S], F32R, at)
        k_ho = sb("k_ho", [MROW + 12, 2, S], F32R, at)
        v_hi = sb("v_hi", [P, 2, NS, 66], F32R, at)
        v_lo = sb("v_lo", [P, 2, NS, 66], F32R, at)
        over_pn = ExitStack()
        x_blk = sb("x_blk", [P, CMP_L, N_CMP], F32, over_pn)
        over_pn.close()
        pn = sb("pn", [P, NS, 384], F32, at)
        kc_hl = sb("kc_hl", [P, P], F32R, at)
        kc_ho = sb("kc_ho", [MROW + 12, P], F32R, at)
        vc_hi = sb("vc_hi", [P, 66], F32R, at)
        vc_lo = sb("vc_lo", [P, 66], F32R, at)
        p_f = sb("p_f", [P, 2, HALF], F32, at)
        p_hi = sb("p_hi", [P, 3, HALF], F32R, at)
        p_lo = sb("p_lo", [P, 3, HALF], F32R, at)
        o_T = sb("o_T", [66, 2, HALF], F32, at)
        mix_s = sb("mix_s", [P, 2, 384], F32, at)
        part = sb("part", [P, 2, 12, 2], F32, at)
        m_raw = sb("m_raw", [P, 2, 12], F32, at)
        m_neg = sb("m_neg", [P, 2, 12], F32R, at)
        fin = sb("fin", [P, 2, 3, 4], F32, at)
        fin_t = sb("fin_t", [P, 4, HD], F32, at)
        es = sb("es", [P, 8, 2, 3], F32, at)
        comb = sb("comb", [P, 8, 6], F32, at)
        rope_t = sb("rope_t", [P, 2, 320], F32, at)
        cmpx = ExitStack()
        cv_T = sb("cv_T", [P, S], F32, cmpx)
        w_cmp = sb("w_cmp", [P, CMP_L, HD], F32, cmpx)
        cmpx.close()
        u_T2 = sb("u_T2", [66, 2, S], F32, cmpx)
        v_perm = sb("v_perm", [P, NS, P], F32, cmpx)
        cmpx.close()
        at.close()
        u_T = [u_T0, u_T1, u_T2]
        nat = ExitStack()
        xn = sb("xn", [P, NS, D], F32, nat)
        yn = sb("yn", [P, NS, D], F32, nat)
        junk = sb("junk", [P, D], F32, nat)
        lo_t = sb("lo_t", [P, 2, HALF], F32, nat)
        ada_acc = sb("ada_acc", [P, 4 * D], F32, nat)
        sb("past_ff", [P, 8], F32, nat)
        g_b = sb("g_b", [P, 2, D], F32, nat)
        NADA, ADAW = 4, D
        ada_raw = sb("ada_raw", [P, NADA, ADAW], F32, nat)
        nat.close()
        ada = ExitStack()
        sb("xn_place", [P, NS, D], F32, ada)
        ang = sb("ang", [P, 4, NS * 32], F32, ada)
        pos_i = sb("pos_i", [P, NS], I32, ada)
        pos_f = sb("pos_f", [P, NS], F32, ada)
        inv_f = sb("inv_f", [P, 32], F32, ada)
        cc = sb("cc", [P, 3, KT_D], F32, ada)
        ada.close()
        ff = ExitStack()
        a_hi = sb("a_hi", [P, 2, 2, S], F32R, ff)
        a_lo = sb("a_lo", [P, 2, 2, S], F32R, ff)
        sb("yn_place", [P, NS, D], F32, ff)
        gs = sb("gs", [P, 2, S + 2], F32, ff)
        us = sb("us", [P, 2, S], F32, ff)
        ct = sb("ct", [P, 2, S], F32, ff)
        ff.close()
        PS = [ctx.enter_context(nc.psum_tensor(f"bank{i}", [P, HALF], F32)) for i in range(8)]

        MASKS = {"C": fc_S[:, 1, :], "F": fc_S[:, 0, :], "E": e_S[:, :], "B": b_S[:, :]}
        MASKS_T = {"CT": strip_T[:, 1, :], "ET": edge_T[:, :],
                   "CT|FT": strip_T[:, 1:3, :], "|CT": strip_T[:, 0:2, :], "FT|": strip_T[:, 2:4, :],
                   "BT|": strip_BT[:, 1:3, :], "|BT": strip_BT[:, 0:2, :]}

        def f32(ap):
            return ap.bitcast(F32)

        def bc(ap, shape):
            return ap.to_broadcast(shape)

        NWT = len(plan.tiles)
        raw_at, tot = [], [0] * NRAW
        for w, t in enumerate(plan.tiles):
            nd = {"gu": 2}.get(t["spec"][0], len(t["spec"][2]) if t["spec"][0] != "gu" else 2)
            tot[w % NRAW] += 16 * nd
            raw_at.append(tot[w % NRAW])
        used_at, used = [], 0
        for t in plan.tiles:
            last = t is plan.tiles[t["p"]["w0"] + t["p"]["n"] - 1]
            used += not last
            used_at.append(None if last else used)
        NBANK = 8 * len(plan.passes)
        ev_a = ev_v = 0
        for p in plan.passes:
            p["a0"], p["v0"] = ev_a, ev_v
            if p["kind"] == "dn":
                ev_v += 8
            else:
                ev_a += 8
        NEV_A, NEV_V = ev_a, ev_v
        NU, NC_, NT_, NSUB = plan.n["unit"], plan.n["chunk"], plan.n["task"], plan.n["sub"]
        NJ = plan.jobs
        dist_list = [(st, d) for st in plan.stages for d in st["dists"]]
        dtr = 0
        tsub = 0
        vsp = 0
        for st, d in dist_list:
            for j in d["jobs"]:
                dtr += j["what"] in "QK"
                j["dve_after"] = dtr
            vsp += bool(d["lay"]["values"])
            d["v_after"] = vsp
        NDTR, NVS = dtr, vsp
        t_no = 0
        mixn = 0
        for st in plan.stages:
            for kind, o in st["steps"]:
                if kind == "T" and st["kind"] != "B":
                    o["t_no"] = t_no
                    t_no += 1
                    if st["kind"] == "C" or o["br"] == 2:
                        o["mix_no"] = mixn
                        mixn += 1
        bc_mix0 = mixn
        mixn += NS
        NTF, NMIX = t_no, mixn
        es_no = 0
        for st in plan.stages:
            if st["kind"] == "C":
                for kind, o in st["steps"]:
                    if kind == "M":
                        o["es_no"] = es_no
                        es_no += 1
        NES = es_no
        NTT = 3 * 2 * KT_D
        ADA_PARTS = [dict(c0=0, nj=2, a0=0), dict(c0=2 * D, nj=4, a0=2 * KT_D)]
        NA_TILES = 6 * KT_D

        ld_c = sem("ld_c")
        ld_par = sem("ld_par")
        ld_bias = sem("ld_bias")
        ada_full = [sem(f"ada_full{i}") for i in range(NADA)]
        ada_used = sem("ada_used")
        ada_zero = sem("ada_zero")
        ada_sums = sem("ada_sums")
        ada_done = sem("ada_done")
        ld_cmp = sem("ld_cmp")
        ld_nw = sem("ld_nw")
        w_full = [sem(f"w_full{i}") for i in range(NRAW)]
        w_split = sem("w_split")
        w_used = sem("w_used")
        bank_full = sem("bank_full")
        evac_a = sem("evac_a")
        evac_v = sem("evac_v")
        consts = sem("consts")
        attn_init = sem("attn_init")
        x_ld = [sem(f"x_ld{i}") for i in range(NS)]
        squares = sem("squares")
        var_ready = sem("var_ready")
        root_ready = sem("root_ready")
        scaled = sem("scaled")
        tt_full = sem("tt_full")
        tt_act = sem("tt_act")
        tt_dve = sem("tt_dve")
        x_new = sem("x_new")
        x_st = sem("x_st")
        roped = sem("roped")
        tr_full = sem("tr_full")
        tr_act = sem("tr_act")
        tr_dve = sem("tr_dve")
        v_split = sem("v_split")
        v_out = sem("v_out")
        v_back = sem("v_back")
        gate_e = sem("gate_e")
        blocks = sem("blocks")
        cmp_full = sem("cmp_full")
        cmp_act = sem("cmp_act")
        cmp_dve = sem("cmp_dve")
        s_full = sem("s_full")
        s_max = sem("s_max")
        m_ready = sem("m_ready")
        mt_full = sem("mt_full")
        m_rows = sem("m_rows")
        st_full = sem("st_full")
        p_exp = sem("p_exp")
        p_rest = sem("p_rest")
        pv_done = sem("pv_done")
        o_out = sem("o_out")
        t_full = sem("t_full")
        t_done = sem("t_done")
        sink_d = sem("sink_d")
        sink_e = sem("sink_e")
        bc_full = sem("bc_full")
        bc_d = sem("bc_d")
        bc_e = sem("bc_e")
        bc_done = sem("bc_done")
        mix_st = [sem(f"mix_st{i}") for i in range(2)]
        conv_s = sem("conv_s")
        conv_d = sem("conv_d")
        gelu_s = sem("gelu_s")
        gate_d = sem("gate_d")
        act_h = sem("act_h")
        act_l = sem("act_l")
        act_c = sem("act_c")
        dve_c = sem("dve_c")
        pool_c = sem("pool_c")
        rope_tab = sem("rope_tab")
        rope_sin = sem("rope_sin")
        cond_e = sem("cond_e")

        class Chain:

            def __init__(self, eng, s):
                self.eng, self.s, self.n = eng, s, 0
                self.base = 0

            def loop(self, L, each):
                self.base, self.n, self.each = L * each + self.n, 0, each

            def close(self):
                assert self.n == self.each, self.n

            def tick(self, ins):
                ins.then_inc(self.s, 1)
                self.n += 1

            def sync(self):
                self.eng.wait_ge(self.s, self.base + self.n)

            def link(self, ins):
                self.tick(ins)
                self.sync()

        block = ctx.enter_context(nc.Block())

        def perm(ap, kv, s):
            if kv == 0:
                return ap[:, s * P:(s + 1) * P]
            dil = 4 if kv == 1 else 16
            n = P // dil
            return ap.rearrange("p (c n) -> p n c", c=dil)[:, s * n:(s + 1) * n, :]

        @block.sync
        def _(sp):
            sp.dma_start(cond[:, :], c[0].rearrange("(k p) -> p k", p=P), allow_slow_non_contiguous=True).then_inc(ld_c, 16)
            sp.dma_start(pos_i[:, :], positions[0].rearrange("(s p) -> p s", p=P), allow_slow_non_contiguous=True).then_inc(ld_c, 16)

            def weight(L, w):
                t = plan.tiles[w]
                spec = t["spec"]
                if w >= NRAW:
                    sp.wait_ge(w_split, L * NWT + w - NRAW + 1)
                    sp.nop(nofuse=True)
                slot = w_raw[:, w % NRAW, :]
                full = w_full[w % NRAW]
                if spec[0] == "gu":
                    _, k, g = spec
                    for m, wt in enumerate((w_gate, w_up)):
                        sp.dma_start(slot[:, m * 2 * P:(m + 1) * 2 * P],
                                     wt[L, k * P:(k + 1) * P, g * 2 * P:(g + 1) * 2 * P]).then_inc(full, 16)
                else:
                    name, k, cols = spec
                    wt = {"w_in": w_in, "w_out": w_out, "w_down": w_down}[name]
                    at_ = 0
                    for c0, n in cols:
                        sp.dma_start(slot[:, at_:at_ + n], wt[L, k * P:(k + 1) * P, c0:c0 + n]).then_inc(full, 16)
                        at_ += n

            def mix_store(L, n, i, c0, width):
                sp.dma_start(mix_dram[i * P:(i + 1) * P, c0:c0 + width], mix_s[:, n % 2, 0:width])\
                  .then_inc(mix_st[n % 2], 16)

            def ada_load(L, part, a):
                k, j = divmod(a, part["nj"])
                n = part["a0"] + a
                if n >= NADA:
                    sp.wait_ge(ada_used, L * NA_TILES + n - NADA + 1)
                    sp.nop(nofuse=True)
                c0 = part["c0"] + j * ADAW
                sp.dma_start(ada_raw[:, n % NADA, :], w_ada[L, k * P:(k + 1) * P, c0:c0 + ADAW])\
                  .then_inc(ada_full[n % NADA], 16)

            for s in range(NS):
                sp.dma_start(xn[:, s, :], x2[s * P:(s + 1) * P, :]).then_inc(x_ld[s], 16)
            sp.dma_start(out2, x2).then_inc(x_st, 16)

            with sp.Fori(0, DEPTH) as L:
                for a in range(NADA):
                    ada_load(L, ADA_PARTS[0], a)
                par = [(nw_col[:, 0, :], norm_w[L, 0].rearrange("(k p) -> p k", p=P)),
                       (nw_col[:, 1, :], norm_w[L, 2].rearrange("(k p) -> p k", p=P)),
                       (sink_b[:, 0, :], sinks[bass.ts(L, 1), :].to_broadcast([P, 6])),
                       (pe_col[0:HD, :], cmp_pe_k[L].rearrange("l d -> d l")),
                       (pe_col[HD:P, :], cmp_pe_v[L].rearrange("l d -> d l")),
                       (cb[:, :], conv_b[L].rearrange("(t p) -> p t", p=P))]
                par += [(cw[:, i, :], conv_w[L, i].rearrange("(t p) -> p t", p=P)) for i in range(3)]
                for o_, i_ in par:
                    sp.dma_start(o_, i_, allow_slow_non_contiguous=True).then_inc(ld_par, 16)
                sp.wait_ge(ada_zero, 2 * L + 1)
                sp.nop(nofuse=True)
                sp.dma_start(ada_acc[0:1, 0:2 * D], b_ada[bass.ts(L, 1), 0:2 * D]).then_inc(ld_bias, 16)
                for a in range(NADA, 2 * KT_D):
                    ada_load(L, ADA_PARTS[0], a)
                wn = 0
                for _ in range(NRAW):
                    weight(L, wn)
                    wn += 1
                sp.wait_ge(ada_used, L * NA_TILES + 2 * KT_D)
                sp.nop(nofuse=True)
                for o_, i_ in ((w_cmp[0:HD, :, :], cmp_w_k[L].rearrange("l d e -> d l e")),
                               (w_cmp[HD:P, :, :], cmp_w_v[L].rearrange("l d e -> d l e"))):
                    sp.dma_start(o_, i_, allow_slow_non_contiguous=True).then_inc(ld_cmp, 16)
                for st in plan.stages:
                    for d in st["dists"]:
                        end = d["pass"]["w0"] + d["pass"]["n"]
                        while wn < end:
                            weight(L, wn)
                            wn += 1
                        if st["kind"] == "B" and st["kv"]:
                            sp.wait_ge(evac_a, L * NEV_A + d["pass"]["a0"] + 8)
                            sp.nop(nofuse=True)
                            for s in range(NS):
                                sp.dma_start(v_dram[s * P:(s + 1) * P, :], pn[:, s, 256:384]).then_inc(v_out, 16)
                            n = L * 2 + st["kv"]
                            sp.wait_ge(v_out, 16 * NS * n)
                            sp.nop(nofuse=True)
                            for i in range(NS):
                                if st["kv"] == 1:
                                    v = v_dram.rearrange("(n c) d -> c n d", c=4)
                                    sp.dma_start(v_perm[:, i, :], v[i // 2, (i % 2) * P:(i % 2 + 1) * P, :]).then_inc(v_back, 8 * 2)
                                else:
                                    v = v_dram.rearrange("(n c) d -> c n d", c=16)
                                    for b in range(2):
                                        sp.dma_start(v_perm[b * 64:(b + 1) * 64, i, :], v[2 * i + b]).then_inc(v_back, 16)
                    for _ in range(NRAW):
                        weight(L, wn)
                        wn += 1
                    if st["kind"] != "B":
                        for kind, o in st["steps"]:
                            if kind == "T" and "mix_no" in o:
                                sp.wait_ge(t_done, L * NTF + o["t_no"] + 1)
                                sp.nop(nofuse=True)
                                c0, width = (0, 256) if st["kind"] == "A" else (640 + 192 * st["kv"], 192)
                                mix_store(L, o["mix_no"], o["task"]["i"], c0, width)
                for s in range(NS):
                    sp.wait_ge(bc_done, L * NS + s + 1)
                    sp.nop(nofuse=True)
                    mix_store(L, bc_mix0 + s, s, 256, 384)
                for i in range(2):
                    sp.wait_ge(mix_st[i], (L + 1) * (16 * NMIX // 2))
                    sp.nop(nofuse=True)
                for s in range(NS):
                    sp.dma_start(xn[:, s, :], mix_dram[s * P:(s + 1) * P, :]).then_inc(x_ld[s], 16)
                sp.wait_ge(ada_zero, 2 * L + 2)
                sp.nop(nofuse=True)
                sp.dma_start(ada_acc[0:1, :], b_ada[bass.ts(L, 1), 2 * D:6 * D]).then_inc(ld_bias, 16)
                for i in range(2):
                    sp.dma_start(g_b[:, i, :], norm_w[bass.ts(L, 1), 1 + 2 * i, :].to_broadcast([P, D])).then_inc(ld_nw, 16)
                a = 0
                while wn < plan.out_pass[1]["w0"] + KT_D or a < 4 * KT_D:
                    for _ in range(3):
                        if a < 4 * KT_D:
                            ada_load(L, ADA_PARTS[1], a)
                            a += 1
                    if wn < plan.out_pass[1]["w0"] + KT_D:
                        weight(L, wn)
                        wn += 1
                sp.wait_ge(tt_full, (L * 3 + 2) * 16)
                sp.nop(nofuse=True)
                for s in range(NS):
                    sp.dma_start(xn[:, s, :], out2[s * P:(s + 1) * P, :]).then_inc(x_ld[s], 16)
                for _ in range(NRAW):
                    weight(L, wn)
                    wn += 1
                for s in range(NS):
                    sp.wait_ge(x_new, (2 * L + 1) * NS + s + 1)
                    sp.nop(nofuse=True)
                    sp.dma_start(out2[s * P:(s + 1) * P, :], xn[:, s, :]).then_inc(x_st, 16)
                while wn < NWT:
                    weight(L, wn)
                    wn += 1
                sp.wait_ge(x_st, L * (16 * 2 * NS) + 16 * NS + 16)
                sp.nop(nofuse=True)
                sp.wait_ge(bank_full, (L + 1) * NBANK)
                sp.nop(nofuse=True)
                for s in range(NS):
                    sp.dma_start(xn[:, s, :], out2[s * P:(s + 1) * P, :]).then_inc(x_ld[s], 16)
                for s in range(NS):
                    sp.wait_ge(x_new, (2 * L + 2) * NS + s + 1)
                    sp.nop(nofuse=True)
                    sp.dma_start(out2[s * P:(s + 1) * P, :], xn[:, s, :]).then_inc(x_st, 16)
            sp.wait_ge(x_st, 16 * 2 * NS * DEPTH + 16)

        @block.gpsimd
        def _(pool):
            ch = Chain(pool, pool_c)
            for m in (ident, ident_b):
                ch.link(nc.gpsimd.memset(m[:, :], 0.0))
                ch.tick(nc.gpsimd.affine_select(out=m[:, :], in_=m[:, :], compare_op=ALU.not_equal, fill=1.0, base=0,
                                                pattern=[[-1, P]], channel_multiplier=1))
            ch.tick(nc.gpsimd.memset(ones[:, :], 1.0))
            for m in (strip_T, strip_BT):
                ch.tick(nc.gpsimd.memset(m[:, :, :], NEG))
            zero = [strip_T[:, 1, :], strip_T[:, 2, :], strip_BT[:, 1, :], edge_T[:, :], cmp_T[:, :], fc_S[:, 0, :],
                    fc_S[:, 1, :], e_S[:, :], b_S[:, :], cmp_S[:, :], lane_mask[:, :, :]]
            ch.sync()
            for m in zero:
                ch.tick(nc.gpsimd.memset(m, 0.0))
            ch.tick(nc.gpsimd.memset(row_ones[:, :], 1.0))
            ch.tick(nc.gpsimd.memset(f32(sel_m[:, :]), 0.0))
            ch.sync()

            def keep(m, cmp, base, cm, pattern, fill=NEG):
                ch.tick(nc.gpsimd.affine_select(out=m, in_=m, compare_op=cmp, fill=fill, base=base, pattern=pattern,
                                                channel_multiplier=cm))

            one = [[1, P]]
            neg = [[-1, P]]
            keep(strip_T[:, 1, :], ALU.is_ge, 0, -1, one)
            keep(strip_T[:, 2, :], ALU.is_ge, 0, 1, neg)
            keep(edge_T[:, :], ALU.is_gt, 0, 1, neg)
            keep(strip_BT[:, 1, :], ALU.is_ge, 0, -1, one)
            keep(cmp_T[:, :], ALU.is_ge, -(CMP_L - 1), -16, [[1, S]])
            keep(fc_S[:, 0, :], ALU.is_ge, 0, -1, one)
            keep(fc_S[:, 1, :], ALU.is_ge, 0, 1, neg)
            keep(e_S[:, :], ALU.is_gt, 0, -1, one)
            keep(b_S[:, :], ALU.is_ge, 0, 1, neg)
            keep(cmp_S[:, :], ALU.is_ge, 16 * CMP_OFF - (CMP_L - 1), 1, [[-16, CMP_OFF + P]])
            keep(row_ones[:, :], ALU.is_ge, 0, 1, [[-4, 3]], 0.0)
            ch.sync()
            keep(strip_BT[:, 1, 64:P], ALU.is_ge, -64, 1, [[0, 64]])
            keep(b_S[:, 0:64], ALU.is_ge, 63, -1, [[0, 64]])
            keep(row_ones[:, :], ALU.is_ge, 3, -1, [[4, 3]], 0.0)
            for br in range(3):
                keep(lane_mask[:, :, :], ALU.not_equal, -4 * br, 1, [[-1, 4], [0, P]], 1.0)
                ch.sync()
            nc.gpsimd.memset(f32(sel_m[MROW:MROW + 4, 65:66]), -1.0).then_inc(consts, 1)
            pool.wait_ge(consts, 1)

            def split(L, w):
                t = plan.tiles[w]
                n = t["width"]
                pool.wait_ge(w_full[w % NRAW], L * tot[w % NRAW] + raw_at[w])
                back = w - NW
                if back >= 0:
                    if used_at[back] is not None:
                        pool.wait_ge(w_used, L * used + used_at[back])
                    else:
                        pool.wait_ge(bank_full, L * NBANK + 8 * (plan.tiles[back]["p"]["ord"] + 1))
                pool.nop(nofuse=True)
                src = w_raw[:, w % NRAW, 0:n]
                ch.link(nc.gpsimd.tensor_copy(w_hi[:, w % NW, 0:n], src))
                nc.gpsimd.tensor_tensor(w_lo[:, w % NW, 0:n], src, f32(w_hi[:, w % NW, 0:n]), ALU.subtract)\
                  .then_inc(w_split, 1)

            with pool.Fori(0, DEPTH) as L:
                ch.loop(L, POOL_STEPS)
                for w in range(NW):
                    split(L, w)
                pool.wait_ge(tt_dve, (L * 3 + 1) * 16)
                pool.nop(nofuse=True)
                for m, val in ((v_hi[:, :, :, 64:65], 1.0), (v_hi[:, :, :, 65:66], 0.0), (v_lo[:, :, :, 64:66], 0.0),
                               (kc_hl[:, :], 0.0), (kc_ho[:, :], 0.0), (vc_hi[:, 0:64], 0.0), (vc_hi[:, 64:65], 1.0),
                               (vc_hi[:, 65:66], 0.0)):
                    ch.tick(nc.gpsimd.memset(f32(m), val))
                nc.gpsimd.memset(f32(vc_lo[:, :]), 0.0).then_inc(attn_init, 1)
                w = NW
                for st, d in dist_list:
                    while w < d["pass"]["w0"] + d["pass"]["n"] :
                        split(L, w)
                        w += 1
                    for _ in range(NW):
                        split(L, w)
                        w += 1
                    if d["lay"]["values"]:
                        if st["kind"] == "B" and st["kv"]:
                            k = NS if st["kv"] == 1 else 3 * NS
                            pool.wait_ge(v_back, 16 * (L * 3 * NS + k))
                            src = v_perm[:, :, :]
                            off = 256
                        else:
                            src, off = pn[:, :, :], 0
                        pool.wait_ge(evac_a, L * NEV_A + d["pass"]["a0"] + 8)
                        pool.nop(nofuse=True)
                        for c0, slot in d["lay"]["values"]:
                            ch.tick(nc.gpsimd.tensor_copy(v_hi[:, slot, :, 0:HD], src[:, :, c0 - off:c0 - off + HD]))
                        ch.sync()
                        vs = d["lay"]["values"]
                        for c0, slot in vs:
                            ins = nc.gpsimd.tensor_tensor(v_lo[:, slot, :, 0:HD], src[:, :, c0 - off:c0 - off + HD],
                                                          f32(v_hi[:, slot, :, 0:HD]), ALU.subtract)
                            if slot == vs[-1][1]:
                                ins.then_inc(v_split, 1)
                            else:
                                ch.tick(ins)
                while w < NWT:
                    split(L, w)
                    w += 1
                ch.close()

        @block.tensor
        def _(pe):
            mm = nc.tensor.matmul
            pe.wait_ge(consts, 1)

            def run_pass(L, p, bufs=0):
                kind = p["kind"]
                for k in range(p["n"]):
                    w = p["w0"] + k
                    pe.wait_ge(w_split, L * NWT + w + 1)
                    hi, lo = w_hi[:, w % NW, :], w_lo[:, w % NW, :]
                    for b in range(8):
                        if k == 0:
                            bank_free(L, p, b)
                        first, last = k == 0, k == p["n"] - 1
                        if kind == "gu":
                            j, m, h = b // 4, b // 2 % 2, b % 2
                            cs = slice(m * 2 * P + j * P, m * 2 * P + (j + 1) * P)
                            rs = slice(h * HALF, (h + 1) * HALF)
                            prods = [(hi[:, cs], hT_hi[:, k, rs]), (hi[:, cs], hT_lo[:, k, rs]),
                                     (lo[:, cs], hT_hi[:, k, rs])]
                            o_ = PS[b][:, :]
                        else:
                            a, al = (a_hi[:, bufs, k], a_lo[:, bufs, k]) if kind == "dn" else (hT_hi[:, k], hT_lo[:, k])
                            qs = slice(b * P, (b + 1) * P)
                            n = p["width"]
                            prods = [(a[:, qs], hi[:, 0:n]), (a[:, qs], lo[:, 0:n]), (al[:, qs], hi[:, 0:n])]
                            o_ = PS[b][:, 0:n]
                        for x, (l_, r_) in enumerate(prods):
                            ins = mm(o_, l_, r_, start=first and x == 0, stop=last and x == 2)
                        if last:
                            ins.then_inc(bank_full, 1)
                    if not last:
                        ins.then_inc(w_used, 1)

            def bank_free(L, p, b):
                prev = plan.passes[p["ord"] - 1] if p["ord"] else None
                if prev is not None and prev["kind"] == "dn":
                    pe.wait_ge(evac_v, L * NEV_V + prev["v0"] + b + 1)
                elif prev is not None:
                    pe.wait_ge(evac_a, L * NEV_A + prev["a0"] + b + 1)

            def columns(L, bank, j0):
                for x in range(2 * KT_D):
                    ins = mm(bank[:, x:x + 1], ada_acc[:, j0 + x * P:j0 + (x + 1) * P], ones[:, 0:1], start=True, stop=True)
                return ins

            def turned(L, site):
                for j in range(16):
                    if site == 0 and j == 7:
                        pe.wait_ge(ada_used, L * NA_TILES + 2 * KT_D)
                        columns(L, PS[7], 0).then_inc(ada_sums, 1)
                        pe.wait_ge(ada_done, 2 * L + 1)
                    k, h = divmod(j, 2)
                    n = (L * 3 + site) * 16 + j
                    if j >= 8:
                        pe.wait_ge(tt_act, n - 7)
                        pe.wait_ge(tt_dve, n - 7)
                    for t in range(4):
                        s = 4 * h + t
                        if k == 0:
                            if site == 1:
                                pe.wait_ge(x_ld[s], 16 * (3 * L + 2))
                            else:
                                pe.wait_ge(scaled, (2 * L + (site == 2)) * NS + s + 1)
                        ins = mm(PS[j % 8][:, t * P:(t + 1) * P], xn[:, s, k * P:(k + 1) * P], ident[:, :],
                                 start=True, stop=True, is_transpose=True)
                    ins.then_inc(tt_full, 1)

            def dist(L, st, d):
                base = L * NJ
                for j in d["jobs"]:
                    n = j["ord"]
                    if j is d["jobs"][0]:
                        pe.wait_ge(evac_a, L * NEV_A + d["pass"]["a0"] + 4)
                    x = d["jobs"].index(j)
                    if x >= 4:
                        old = d["jobs"][x - 4]
                        pe.wait_ge(tr_act, base + old["ord"] + 1)
                        pe.wait_ge(tr_dve, L * NDTR + old["dve_after"])
                    for t in range(4):
                        s = 4 * j["half"] + t
                        if j["what"] in ("Q", "K", "KC"):
                            pe.wait_ge(roped, (L * plan.proj + d["ord"]) * NS + s + 1)
                        else:
                            pe.wait_ge(evac_a, L * NEV_A + d["pass"]["a0"] + s + 1)
                        pe.nop(nofuse=True)
                        src = pn[:, s, j["col"]:j["col"] + HD]
                        ins = mm(PS[x % 4][0:HD, t * P:(t + 1) * P], src, ident[:, :], start=True, stop=True,
                                 is_transpose=True)
                    ins.then_inc(tr_full, 1)

            def compress(L):
                pe.wait_ge(blocks, L + 1)
                pe.wait_ge(ld_cmp, 32 * (L + 1))
                pe.nop(nofuse=True)
                for l_ in range(CMP_L):
                    mm(PS[4][0:HD, 0:N_CMP], w_cmp[0:HD, l_, :], x_blk[0:HD, l_, :], start=l_ == 0, stop=l_ == CMP_L - 1)
                for l_ in range(CMP_L):
                    ins = mm(PS[5][0:N_CMP, 0:HD], x_blk[HD:P, l_, :], w_cmp[HD:P, l_, :],
                             start=l_ == 0, stop=l_ == CMP_L - 1)
                ins.then_inc(cmp_full, 1)

            def step(L, st, kind, o):
                if kind == "S":
                    n = L * NC_ + o["ord"]
                    if o["ord"] >= 2:
                        pe.wait_ge(s_max, n - 1)
                    slot, q0 = o["lhs"]
                    keys = kc_hl[:, :] if o["kv"] == "cmp" else k_hl[:, o["kv"], o["key0"]:o["key0"] + o["cols"]]
                    bank = PS[o["ord"] % 2]
                    ins = mm(bank[:, 0:o["cols"]], q_hh[:, slot, q0:q0 + P], keys, start=True, stop=not o["masks"],
                             skip_group_check=True)
                    for x, (m, off) in enumerate(o["masks"]):
                        if isinstance(m, tuple):
                            a = CMP_OFF - 8 * m[1]
                            src = cmp_S[:, a:a + P]
                        else:
                            src = MASKS[m]
                        ins = mm(bank[:, off:off + P], ident_b[:, :], src, start=False,
                                 stop=x == len(o["masks"]) - 1, skip_group_check=True)
                    ins.then_inc(s_full, 1)
                elif kind == "MT":
                    n = L * NT_ + o["ord"]
                    pe.wait_ge(m_ready, n + 1)
                    if o["ord"]:
                        pe.wait_ge(m_rows, n)
                    mm(PS[7][0:o["rows"], 0:P], f32(m_neg[:, o["ord"] % 2, 0:o["rows"]]), ident[:, :],
                       start=True, stop=True, is_transpose=True).then_inc(mt_full, 1)
                elif kind == "ST":
                    n = L * NU + o["ord"]
                    if o["ord"] >= 2:
                        pe.wait_ge(p_exp, n - 1)
                    if o["sub"]["units"][0] is o:
                        pe.wait_ge(m_rows, L * NT_ + o["task"]["ord"] + 1)
                    bank = PS[2 + o["ord"] % 2]
                    K2 = MROW + o["task"]["rows"]
                    gs_ = o["groups"]
                    first = True
                    for g_ in gs_:
                        kv = g_.get("kv", o["kv"])
                        q0, nq = g_["q"]
                        w = nq * g_["n"]
                        ks = slice(o["key"] * P, (o["key"] + 1) * P)
                        k1, k2 = (kc_hl[:, :], kc_ho[0:K2, :]) if kv == "cmp" else (k_hl[:, kv, ks], k_ho[0:K2, kv, ks])
                        cs = slice(g_["q0"], g_["q0"] + g_["n"])
                        o_ = bank[:, g_["out"]:g_["out"] + w]
                        mm(o_, k1, q_hh[:, q0:q0 + nq, cs], start=first, stop=False, skip_group_check=True)
                        first = False
                        ins = mm(o_, k2, q_lm[0:K2, q0:q0 + nq, cs], start=False,
                                 stop=g_ is gs_[-1] and o["mask"] is None, skip_group_check=True)
                    if o["mask"] is not None:
                        m = o["mask"]
                        if isinstance(m, tuple):
                            src = cmp_T[:, m[1] * P:(m[1] + 1) * P].unsqueeze(1).to_broadcast([P, 4, P])
                        elif "|" in m:
                            src = MASKS_T[m].unsqueeze(1).to_broadcast([P, 2, 2, P])
                        else:
                            src = MASKS_T[m].unsqueeze(1).to_broadcast([P, o["task"]["lanes"], P])
                        ins = mm(bank[:, 0:o["task"]["lanes"] * P], ident_b[:, :], src, start=False, stop=True,
                                 skip_group_check=True)
                    ins.then_inc(st_full, 1)
                elif kind == "PV":
                    n = L * NU + o["ord"]
                    s = o["sub"]
                    pe.wait_ge(p_rest, n + 1)
                    bank = PS[4 + s["ord"] % 2]
                    if o["first"] and s["ord"] >= 2:
                        pe.wait_ge(o_out, L * NSUB + s["ord"] - 1)
                    ph, pl = p_hi[:, o["ord"] % 3, :], p_lo[:, o["ord"] % 3, :]
                    gs_ = o["groups"]
                    start = o["first"]
                    for g_ in gs_:
                        kv = g_.get("kv", o["kv"])
                        w = g_["q"][1] * g_["n"]
                        cs = slice(g_["out"], g_["out"] + w)
                        vh, vl = (vc_hi[:, :], vc_lo[:, :]) if kv == "cmp" else (v_hi[:, kv, o["key"], :], v_lo[:, kv, o["key"], :])
                        for x, (l_, r_) in enumerate(((vh, ph), (vh, pl), (vl, ph))):
                            stop = o["last"] and g_ is gs_[-1] and x == 2 and st["kind"] != "B"
                            ins = mm(bank[0:66, cs], l_, r_[:, cs], start=start, stop=stop, skip_group_check=True)
                            start = False
                    ins.then_inc(pv_done, 1)
                    if o["last"] and st["kind"] == "B":
                        g0 = o["task"]["i"] * 2 * P
                        for g_ in gs_:
                            cs = slice(g_["out"], g_["out"] + 2 * P)
                            ins = mm(bank[0:66, cs], sel_m[MROW:MROW + 4, :], q_lm[MROW:MROW + 4, g_["q"][0], g0:g0 + 2 * P],
                                     start=False, stop=g_ is gs_[-1], skip_group_check=True)
                        ins.then_inc(cmp_full, 1)
                elif kind == "T" and st["kind"] != "B":
                    n = L * NTF + o["t_no"]
                    pe.wait_ge(o_out, L * NSUB + o["ord"] + 1)
                    if o["t_no"]:
                        pe.wait_ge(t_done, n)
                    for l_ in range(o["task"]["lanes"]):
                        ins = mm(PS[6][:, l_ * 66:(l_ + 1) * 66], o_T[:, o["ord"] % 2, l_ * P:(l_ + 1) * P],
                                 ident[0:66, 0:66], start=True, stop=True, is_transpose=True)
                    ins.then_inc(t_full, 1)

            def combine(L):
                pe.wait_ge(o_out, (L + 1) * NSUB)
                pe.wait_ge(m_rows, (L + 1) * NT_)
                for s in range(NS):
                    if s >= 2:
                        pe.wait_ge(bc_done, L * NS + s - 1)
                    for x in range(6):
                        ins = mm(PS[6 + s % 2][:, x * 66:(x + 1) * 66], u_T[x // 2][:, x % 2, s * P:(s + 1) * P],
                                 ident[0:66, 0:66], start=True, stop=True, is_transpose=True)
                    ins.then_inc(bc_full, 1)

            def attention_over(L, st):
                last = st["steps"]
                pe.wait_ge(s_max, L * NC_ + max(o["ord"] for k, o in last if k == "S") + 1)
                pe.wait_ge(m_rows, L * NT_ + max(o["ord"] for k, o in last if k == "M") + 1)
                pe.wait_ge(p_exp, L * NU + st["unit1"])
                pe.wait_ge(o_out, L * NSUB + st["sub1"])
                ts = [o["t_no"] for k, o in last if k == "T" and "t_no" in o]
                if ts:
                    pe.wait_ge(t_done, L * NTF + max(ts) + 1)

            with pe.Fori(0, DEPTH) as L:
                turned(L, 0)
                pe.wait_ge(tt_act, (L * 3 + 1) * 16)
                pe.wait_ge(tt_dve, (L * 3 + 1) * 16)
                for st in plan.stages:
                    for d in st["dists"]:
                        run_pass(L, d["pass"])
                        dist(L, st, d)
                        last = d["jobs"][-1]
                        pe.wait_ge(tr_act, L * NJ + last["ord"] + 1)
                        pe.wait_ge(tr_dve, L * NDTR + last["dve_after"])
                    if st["kind"] == "A":
                        pe.wait_ge(attn_init, L + 1)
                        compress(L)
                        pe.wait_ge(cmp_dve, L + 1)
                    pe.wait_ge(v_split, L * NVS + d["v_after"])
                    for kind, o in st["steps"]:
                        step(L, st, kind, o)
                    attention_over(L, st)
                combine(L)
                pe.wait_ge(bc_done, (L + 1) * NS)
                turned(L, 1)
                pe.wait_ge(tt_act, (L * 3 + 2) * 16)
                pe.wait_ge(tt_dve, (L * 3 + 2) * 16)
                for p in plan.out_pass:
                    run_pass(L, p)
                pe.wait_ge(evac_a, L * NEV_A + plan.out_pass[1]["a0"] + 8)
                pe.wait_ge(ada_used, (L + 1) * NA_TILES)
                columns(L, PS[0], D)
                for x in range(4):
                    c0 = (0 if x < 2 else 3) * D + x % 2 * HALF
                    ins = mm(PS[1 + x][:, :], ones[:, :], ada_acc[:, c0:c0 + HALF], start=True, stop=True)
                ins.then_inc(ada_sums, 1)
                pe.wait_ge(ada_done, 2 * L + 2)
                turned(L, 2)
                pe.wait_ge(tt_act, (L * 3 + 3) * 16)
                pe.wait_ge(tt_dve, (L * 3 + 3) * 16)
                run_pass(L, plan.gu[0])
                for g in range(G):
                    if g + 1 < G:
                        run_pass(L, plan.gu[g + 1])
                    pe.wait_ge(act_l, (L * G + g + 1) * 2)
                    for p in plan.dn[g]:
                        run_pass(L, p, g % 2)

        @block.scalar
        def _(act):
            ch = Chain(act, act_c)
            A = nc.scalar.activation
            act.wait_ge(ld_c, 32)
            A(cc[:, 0, :], cond[:, :], ACT.Exp, scale=-1.0).then_inc(cond_e, 1)
            act.wait_ge(rope_tab, 1)
            A(sin_t[:, :, :].rearrange("p a b -> p (a b)"), ang[:, 1, :], ACT.Sin)
            A(cos_t[:, :, :].rearrange("p a b -> p (a b)"), ang[:, 2, :], ACT.Sin).then_inc(rope_sin, 1)

            def root(L, site, src):
                n = L * 4 + site
                for s in range(NS):
                    if site in (0, 2):
                        act.wait_ge(x_new, (2 * L + site // 2) * NS + s + 1)
                    elif site == 3:
                        act.wait_ge(evac_v, L * NEV_V + plan.dn[G - 1][1]["v0"] + s + 1)
                    ch.link(A(junk[:, :], src[:, s, :], ACT.Square, accum_out=stat[:, 0, s:s + 1]))
                A(junk[:, 0:8], stat[:, 0, :], ACT.Copy).then_inc(squares, 1)
                act.wait_ge(var_ready, n + 1)
                ch.link(A(stat[:, 2, :], stat[:, 1, :], ACT.Ln))
                A(stat[:, 3, :], stat[:, 2, :], ACT.Exp, scale=-0.5).then_inc(root_ready, 1)

            def turned(L, site):
                for j in range(16):
                    n = (L * 3 + site) * 16 + j
                    k, h = divmod(j, 2)
                    act.wait_ge(tt_full, n + 1)
                    o_ = hT_hi[:, k, h * HALF:(h + 1) * HALF]
                    if site == 1:
                        A(o_, PS[j % 8][:, :], ACT.Copy).then_inc(tt_act, 1)
                    else:
                        i = site // 2
                        A(o_, PS[j % 8][:, :], ACT.Identity, scale=aff_a[:, i, k:k + 1], bias=aff_b[:, i, k:k + 1])\
                            .then_inc(tt_act, 1)

            def out_of_banks(L, p, dst):
                for b in range(8):
                    act.wait_ge(bank_full, L * NBANK + 8 * p["ord"] + b + 1)
                    A(dst(b), PS[b][:, 0:p["width"]], ACT.Copy).then_inc(evac_a, 1)

            def dist(L, st, d):
                base = L * NJ
                kvp = st["kv"] if st["kind"] == "B" else 0
                for j in d["jobs"]:
                    bank = PS[d["jobs"].index(j) % 4]
                    act.wait_ge(tr_full, base + j["ord"] + 1)
                    h, sl = j["half"], j["slot"]
                    hs = slice(h * HALF, (h + 1) * HALF)

                    def put(dst, src, fn=ACT.Copy):
                        if kvp == 0:
                            return A(dst[:, hs], src, fn)
                        dil = 4 if kvp == 1 else 16
                        m = HALF // dil
                        dv = dst.rearrange("p (c n) -> p n c", c=dil)[:, h * m:(h + 1) * m, :]
                        return A(dv, src.rearrange("p (n c) -> p n c", c=dil), fn)

                    if j["what"] == "Q":
                        ch.tick(put(q_hh[HD:P, sl, :], bank[0:HD, :]))
                        put(q_hh[0:HD, sl, :], bank[0:HD, :]).then_inc(tr_act, 1)
                    elif j["what"] == "K":
                        if h == 0:
                            col = 0 if st["kind"] != "A" else 1 + sl
                            ch.tick(A(k_ho[MROW:MROW + 12, sl, :], row_ones[:, col:col + 1].to_broadcast([12, S]), ACT.Copy))
                        ch.tick(put(k_ho[0:HD, sl, :], bank[0:HD, :]))
                        put(k_hl[0:HD, sl, :], bank[0:HD, :]).then_inc(tr_act, 1)
                    elif j["what"] == "KC":
                        A(cv_T[0:HD, hs], bank[0:HD, :], ACT.Copy).then_inc(tr_act, 1)
                    else:
                        A(cv_T[HD:P, hs], bank[0:HD, :], ACT.Copy).then_inc(tr_act, 1)

            def step(L, st, kind, o):
                if kind == "MT" and st["kind"] == "C":
                    n = L * NES + o["es_no"]
                    act.wait_ge(sink_d, n + 1)
                    A(es[:, o["ord"] % 8, 1, :], es[:, o["ord"] % 8, 0, :], ACT.Exp).then_inc(sink_e, 1)
                elif kind == "ST":
                    n = L * NU + o["ord"]
                    w = o["task"]["lanes"] * P
                    act.wait_ge(st_full, n + 1)
                    bank = PS[2 + o["ord"] % 2]
                    if o["ord"] >= 2:
                        act.wait_ge(p_rest, n - 1)
                    A(p_f[:, o["ord"] % 2, 0:w], bank[:, 0:w], ACT.Exp, scale=SCALE)
                    if o["ord"] >= 3:
                        act.wait_ge(pv_done, n - 2)
                    A(p_hi[:, o["ord"] % 3, 0:w], bank[:, 0:w], ACT.Exp, scale=SCALE).then_inc(p_exp, 1)
                elif kind == "PV" and o["last"]:
                    s = o["sub"]
                    n = L * NSUB + s["ord"]
                    bank = PS[4 + s["ord"] % 2]
                    w = o["task"]["lanes"] * P
                    if st["kind"] == "B":
                        act.wait_ge(cmp_full, L * (1 + 12) + 1 + st["kv"] * 4 + o["task"]["i"] + 1)
                        g0 = o["task"]["i"]
                        for h in range(2):
                            dst = u_T[st["kv"]][:, h, :]
                            src = bank[0:66, h * 2 * P:(h + 1) * 2 * P]
                            if st["kv"] == 0:
                                dst = dst[:, g0 * 2 * P:(g0 + 1) * 2 * P]
                            elif st["kv"] == 1:
                                dst = dst.rearrange("p (n c) -> p c n", c=4)[:, g0, :]
                            else:
                                dst = dst.rearrange("p (n c) -> p c n", c=16)[:, 4 * g0:4 * g0 + 4, :]
                                src = src.rearrange("p (c n) -> p c n", c=4)
                            ins = A(dst, src, ACT.Copy)
                        ins.then_inc(o_out, 1)
                    else:
                        act.wait_ge(pv_done, L * NU + o["ord"] + 1)
                        A(o_T[:, s["ord"] % 2, 0:w], bank[0:66, 0:w], ACT.Copy).then_inc(o_out, 1)

            with act.Fori(0, DEPTH) as L:
                ch.loop(L, ACT_STEPS)
                root(L, 0, xn)
                act.wait_ge(ada_done, 2 * L + 1)
                turned(L, 0)
                for st in plan.stages:
                    for d in st["dists"]:
                        if d["v_after"] - bool(d["lay"]["values"]):
                            act.wait_ge(v_split, L * NVS + d["v_after"] - bool(d["lay"]["values"]))
                        if st["kind"] == "B" and st["kv"] == 2:
                            act.wait_ge(v_out, 16 * NS * (2 * L + 1))
                        out_of_banks(L, d["pass"], lambda b: pn[:, b, 0:d["width"]])
                        if d["width"] == 332:
                            act.wait_ge(evac_a, L * NEV_A + d["pass"]["a0"] + 8)
                            A(gates[:, :, :], pn[:, :, 320:332], ACT.Exp, scale=-1.0).then_inc(gate_e, 1)
                        dist(L, st, d)
                    if st["kind"] == "A":
                        act.wait_ge(cmp_full, L * (1 + 12) + 1)
                        act.wait_ge(attn_init, L + 1)
                        ch.tick(A(kc_ho[MROW:MROW + 12, :], row_ones[:, 0:1].to_broadcast([12, P]), ACT.Copy))
                        ch.tick(A(kc_ho[0:HD, 0:N_CMP], PS[4][0:HD, 0:N_CMP], ACT.Copy))
                        ch.tick(A(kc_hl[0:HD, 0:N_CMP], PS[4][0:HD, 0:N_CMP], ACT.Copy))
                        A(vc_hi[0:N_CMP, 0:HD], PS[5][0:N_CMP, 0:HD], ACT.Copy).then_inc(cmp_act, 1)
                    for kind, o in st["steps"]:
                        step(L, st, kind, o)
                for s in range(NS):
                    act.wait_ge(bc_d, L * NS + s + 1)
                    A(comb[:, 2, :], comb[:, 1, :], ACT.Exp, scale=SCALE).then_inc(bc_e, 1)
                turned(L, 1)
                for n, p in enumerate(plan.out_pass):
                    out_of_banks(L, p, lambda b: yn[:, b, n * HALF:(n + 1) * HALF])
                act.wait_ge(evac_a, L * NEV_A + plan.out_pass[1]["a0"] + 8)
                root(L, 1, yn)
                root(L, 2, xn)
                turned(L, 2)

                def gu(g):
                    if g:
                        act.wait_ge(gate_d, (L * G + g) * 2)
                    out_of_banks(L, plan.gu[g], lambda b: gs[:, b // 4, 2 + b % 2 * HALF:2 + (b % 2 + 1) * HALF]
                                 if b // 2 % 2 == 0 else us[:, b // 4, b % 2 * HALF:(b % 2 + 1) * HALF])
                    act.wait_ge(evac_a, L * NEV_A + plan.gu[g]["a0"] + 8)
                    for j in range(2):
                        f = 2 * g + j
                        if g:
                            act.wait_ge(act_l, (L * G + g - 1) * 2 + j + 1)
                        A(ct[:, j, :], gs[:, j, 2:S + 2], ACT.Identity, scale=cw[:, 2, f:f + 1], bias=cb[:, f:f + 1])\
                            .then_inc(conv_s, 1)
                    for j in range(2):
                        act.wait_ge(conv_d, (L * G + g) * 2 + j + 1)
                        A(ct[:, j, :], ct[:, j, :], ACT.Gelu_apprx_tanh).then_inc(gelu_s, 1)
                    for j in range(2):
                        act.wait_ge(gate_d, (L * G + g) * 2 + j + 1)
                        if g >= 2:
                            act.wait_ge(bank_full, L * NBANK + 8 * (plan.dn[g - 2][1]["ord"] + 1))
                        A(a_hi[:, g % 2, j, :], ct[:, j, :], ACT.Copy).then_inc(act_h, 1)

                for g in range(G):
                    gu(g)
                root(L, 3, yn)
                ch.close()

        @block.vector
        def _(dve):
            ch = Chain(dve, dve_c)
            V = nc.vector
            tt, ts, stt = V.tensor_tensor, V.tensor_scalar, V.scalar_tensor_tensor
            dve.wait_ge(cond_e, 1)
            ch.link(ts(cc[:, 1, :], cc[:, 0, :], 1.0, None, ALU.add))
            ch.link(V.reciprocal(cc[:, 2, :], cc[:, 1, :]))
            ch.link(tt(cond[:, :], cond[:, :], cc[:, 2, :], ALU.mult))
            import math
            for i in range(32):
                ch.tick(V.memset(inv_f[:, i:i + 1], float(THETA ** (-2.0 * i / HD))))
            dve.wait_ge(ld_c, 32)
            ch.link(V.tensor_copy(pos_f[:, :], pos_i[:, :]))
            a3 = ang[:, 0, :].rearrange("p (s i) -> p s i", i=32)
            ch.link(tt(a3, pos_f[:, :].unsqueeze(2).to_broadcast([P, NS, 32]),
                       inv_f[:, :].unsqueeze(1).to_broadcast([P, NS, 32]), ALU.mult))
            BIG = 1.5 * 2 ** 23
            ch.link(ts(ang[:, 1, :], ang[:, 0, :], 1 / (2 * math.pi), BIG, ALU.mult, ALU.add))
            ch.link(ts(ang[:, 1, :], ang[:, 1, :], -BIG, None, ALU.add))
            c1 = 6.28125
            c2 = 1981 / 2 ** 20 + 0.0
            c3 = 2 * math.pi - c1 - c2
            for cn in (c1, c2, c3):
                ch.link(stt(ang[:, 0, :], ang[:, 1, :], -cn, ang[:, 0, :], ALU.mult, ALU.add))
            pi = 3.1415925
            ch.link(ts(ang[:, 1, :], ang[:, 0, :], pi, -pi, ALU.min, ALU.max))
            ch.link(ts(ang[:, 2, :], ang[:, 1, :], -1.0, None, ALU.mult))
            ch.link(tt(ang[:, 2, :], ang[:, 1, :], ang[:, 2, :], ALU.max))
            ts(ang[:, 2, :], ang[:, 2, :], -1.0, math.pi / 2, ALU.mult, ALU.add).then_inc(rope_tab, 1)
            dve.wait_ge(rope_sin, 1)

            def root(L, site):
                n = L * 4 + site
                dve.wait_ge(squares, n + 1)
                ts(stat[:, 1, :], stat[:, 0, :], 1.0 / D, EPS, ALU.mult, ALU.add).then_inc(var_ready, 1)
                dve.wait_ge(root_ready, n + 1)
                ch.link(tt(stat[:, 4, :], stat[:, 1, :], stat[:, 3, :], ALU.mult))
                ch.link(tt(stat[:, 4, :], stat[:, 4, :], stat[:, 3, :], ALU.mult))
                ch.link(ts(stat[:, 4, :], stat[:, 4, :], -0.5, 1.5, ALU.mult, ALU.add))
                ch.link(tt(stat[:, 5, :], stat[:, 4, :], stat[:, 3, :], ALU.mult))

            def scale_rows(L):
                for s in range(NS):
                    ts(xn[:, s, :], xn[:, s, :], stat[:, 5, s:s + 1], None, ALU.mult).then_inc(scaled, 1)

            def turned(L, site):
                for j in range(16):
                    n = (L * 3 + site) * 16 + j
                    k, h = divmod(j, 2)
                    hs = slice(h * HALF, (h + 1) * HALF)
                    dve.wait_ge(tt_act, n + 1)
                    src = PS[j % 8][:, :]
                    if site != 1:
                        i = site // 2
                        ch.tick(ts(lo_t[:, j % 2, :], src, aff_a[:, i, k:k + 1], aff_b[:, i, k:k + 1], ALU.mult, ALU.add))
                        ch.sync()
                        src = lo_t[:, j % 2, :]
                    tt(hT_lo[:, k, hs], src, f32(hT_hi[:, k, hs]), ALU.subtract).then_inc(tt_dve, 1)

            def rope(L, d):
                c0, R, stride = d["lay"]["rope"]
                for s in range(NS):
                    dve.wait_ge(evac_a, L * NEV_A + d["pass"]["a0"] + s + 1)
                    v = pn[:, s, c0:c0 + R * stride if stride == HD else c0 + 192].rearrange("p (r e) -> p r e", e=stride) \
                        if stride == HD else None
                    if v is None:
                        v = pn[:, s, c0:c0 + 2 * stride].rearrange("p (r e) -> p r e", e=stride)[:, :, 0:HD]
                    v = v.rearrange("p r (t i) -> p r t i", t=2)
                    t1 = rope_t[:, 0, 0:R * HD].rearrange("p (r t i) -> p r t i", t=2, i=32)
                    t2 = rope_t[:, 1, 0:R * HD].rearrange("p (r t i) -> p r t i", t=2, i=32)
                    cs = cos_t[:, s, :].unsqueeze(1).unsqueeze(1).to_broadcast([P, R, 2, 32])
                    sn = sin_t[:, s, :].unsqueeze(1).to_broadcast([P, R, 32])
                    ch.tick(tt(t1, v, cs, ALU.mult))
                    ch.tick(tt(t2[:, :, 0, :], v[:, :, 1, :], sn, ALU.mult))
                    ch.tick(tt(t2[:, :, 1, :], v[:, :, 0, :], sn, ALU.mult))
                    ch.sync()
                    ch.tick(tt(v[:, :, 0, :], t1[:, :, 0, :], t2[:, :, 0, :], ALU.subtract))
                    tt(v[:, :, 1, :], t1[:, :, 1, :], t2[:, :, 1, :], ALU.add).then_inc(roped, 1)
                    dve.wait_ge(roped, (L * plan.proj + d["ord"]) * NS + s + 1)

            def dist(L, st, d):
                kvp = st["kv"] if st["kind"] == "B" else 0
                for j in d["jobs"]:
                    if j["what"] not in "QK":
                        continue
                    bank = PS[d["jobs"].index(j) % 4]
                    h, sl = j["half"], j["slot"]
                    dve.wait_ge(tr_act, L * NJ + j["ord"] + 1)

                    def view(t):
                        if kvp == 0:
                            return t[:, h * HALF:(h + 1) * HALF]
                        dil = 4 if kvp == 1 else 16
                        m = HALF // dil
                        return t.rearrange("p (c n) -> p n c", c=dil)[:, h * m:(h + 1) * m, :]

                    def src(ap):
                        return ap if kvp == 0 else ap.rearrange("p (n c) -> p n c", c=4 if kvp == 1 else 16)

                    if j["what"] == "Q":
                        tt(view(q_lm[0:HD, sl, :]), src(bank[0:HD, :]), f32(view(q_hh[0:HD, sl, :])), ALU.subtract)\
                            .then_inc(tr_dve, 1)
                    else:
                        tt(view(k_hl[HD:P, sl, :]), src(bank[0:HD, :]), f32(view(k_hl[0:HD, sl, :])), ALU.subtract)\
                            .then_inc(tr_dve, 1)

            def mix_free(L, n):
                if n >= 2:
                    dve.wait_ge(mix_st[n % 2], L * (16 * NMIX // 2) + 16 * (n // 2))

            def step(L, st, kind, o):
                if kind == "S":
                    n = L * NC_ + o["ord"]
                    dve.wait_ge(s_full, n + 1)
                    V.tensor_reduce(part[:, o["tpar"], o["row"], o["j"]:o["j"] + 1], PS[o["ord"] % 2][:, 0:o["cols"]],
                                    AX.X, ALU.max).then_inc(s_max, 1)
                elif kind == "M":
                    r, par = o["rows"], o["ord"] % 2
                    dve.wait_ge(s_max, L * NC_ + o["chunks"][-1]["ord"] + 1)
                    ch.link(V.tensor_reduce(m_raw[:, par, 0:r], part[:, par, 0:r, :], AX.X, ALU.max))
                    if st["kind"] == "C":
                        q = 3 * st["kv"]
                        ch.link(tt(m_raw[:, par, 0:3], m_raw[:, par, 0:3], sink_b[:, 1, q:q + 3], ALU.max))
                    ts(m_neg[:, par, 0:r], m_raw[:, par, 0:r], -1.0, None, ALU.mult).then_inc(m_ready, 1)
                    ch.link(V.memset(part[:, par, :, :], FLOOR))
                    if st["kind"] == "C":
                        q = 3 * st["kv"]
                        dve.wait_ge(m_ready, L * NT_ + o["ord"] + 1)
                        stt(es[:, o["ord"] % 8, 0, :], f32(m_neg[:, par, 0:3]), SCALE, sink_b[:, 0, q:q + 3], ALU.mult, ALU.add)\
                            .then_inc(sink_d, 1)
                elif kind == "MT":
                    r = o["rows"]
                    dve.wait_ge(mt_full, L * NT_ + o["ord"] + 1)
                    q0 = o["i"] * P
                    if st["kind"] == "B":
                        q0 = o["i"] * 2 * P
                        dst = q_lm[MROW:MROW + 4, BQ:BQ + 2, q0:q0 + 2 * P].rearrange("p h (b q) -> p h b q", b=2)
                        src = PS[7][0:4, 0:P].unsqueeze(1).unsqueeze(1).to_broadcast([4, 2, 2, P])
                        msk = lane_mask[0:4, :, :].rearrange("p (h b) q -> p h b q", h=2)
                    else:
                        n = o["lanes"]
                        dst = q_lm[MROW:MROW + r, 0:n, q0:q0 + P]
                        src = PS[7][0:r, 0:P].unsqueeze(1).to_broadcast([r, n, P])
                        msk = lane_mask[0:r, 0:n, :]
                    tt(dst, src, msk, ALU.mult).then_inc(m_rows, 1)
                elif kind == "R":
                    n = L * NU + o["ord"]
                    w = o["task"]["lanes"] * P
                    dve.wait_ge(p_exp, n + 1)
                    tt(p_lo[:, o["ord"] % 3, 0:w], p_f[:, o["ord"] % 2, 0:w], f32(p_hi[:, o["ord"] % 3, 0:w]), ALU.subtract)\
                        .then_inc(p_rest, 1)
                elif kind == "T" and st["kind"] != "B":
                    dve.wait_ge(t_full, L * NTF + o["t_no"] + 1)
                    n = o["task"]["lanes"]
                    v = PS[6][:, 0:n * 66].rearrange("p (h e) -> p h e", e=66)
                    par = o["ord"] % 2
                    i = o["task"]["i"]
                    s_, r_, w_ = fin[:, par, 0, 0:n], fin[:, par, 1, 0:n], fin[:, par, 2, 0:n]
                    sums = v[:, :, 64:65].rearrange("p h e -> p (h e)")
                    if st["kind"] == "A":
                        ch.link(ts(s_, sums, TINY, None, ALU.max))
                        ch.link(V.reciprocal(r_, s_))
                        g_ = gates[:, i, :].rearrange("p (h b) -> p h b", b=3)[:, :, o["br"]]
                        ch.link(tt(w_, r_, g_, ALU.mult))
                        dst = mix_s[:, i % 2, 0:256].rearrange("p (h e) -> p h e", e=HD)
                        wb = w_.unsqueeze(2).to_broadcast([P, n, HD])
                        if o["br"] == 0:
                            mix_free(L, o["task"]["subs"][2]["mix_no"])
                            tt(dst, v[:, :, 0:HD], wb, ALU.mult).then_inc(t_done, 1)
                            dve.wait_ge(t_done, L * NTF + o["t_no"] + 1)
                        else:
                            ch.link(tt(fin_t[:, :, :], v[:, :, 0:HD], wb, ALU.mult))
                            tt(dst, dst, fin_t[:, :, :], ALU.add).then_inc(t_done, 1)
                            dve.wait_ge(t_done, L * NTF + o["t_no"] + 1)
                    else:
                        dve.wait_ge(sink_e, L * NES + o["task"]["es_no"] + 1)
                        ch.link(tt(s_, sums, es[:, o["task"]["ord"] % 8, 1, :], ALU.add))
                        ch.link(V.reciprocal(r_, s_))
                        mix_free(L, o["mix_no"])
                        dst = mix_s[:, o["mix_no"] % 2, 0:192].rearrange("p (h e) -> p h e", e=HD)
                        tt(dst, v[:, :, 0:HD], r_.unsqueeze(2).to_broadcast([P, n, HD]), ALU.mult).then_inc(t_done, 1)

            def combine(L):
                for s in range(NS):
                    dve.wait_ge(bc_full, L * NS + s + 1)
                    v = PS[6 + s % 2][:, 0:6 * 66].rearrange("p (g h e) -> p g h e", g=3, h=2)
                    m = v[:, :, :, 65]
                    l_ = v[:, :, :, 64]
                    gh = lambda i: comb[:, i, :].rearrange("p (g h) -> p g h", g=3)
                    over_g = lambda i: comb[:, i, :].rearrange("p (g h) -> p h g", g=3)
                    ch.link(V.tensor_reduce(comb[:, 0, 0:2], m.rearrange("p g h -> p h g"), AX.X, ALU.max))
                    tt(gh(1), m, comb[:, 0, 0:2].unsqueeze(1).to_broadcast([P, 3, 2]), ALU.subtract).then_inc(bc_d, 1)
                    dve.wait_ge(bc_e, L * NS + s + 1)
                    ch.link(tt(gh(3), gh(2), l_, ALU.mult))
                    ch.link(V.tensor_reduce(comb[:, 4, 0:2], over_g(3), AX.X, ALU.add))
                    ch.link(V.reciprocal(comb[:, 5, 0:2], comb[:, 4, 0:2]))
                    ch.link(tt(gh(6), gh(2), comb[:, 5, 0:2].unsqueeze(1).to_broadcast([P, 3, 2]), ALU.mult))
                    n = bc_mix0 + s
                    mix_free(L, n)
                    v6 = PS[6 + s % 2][:, 0:6 * 66].rearrange("p (x e) -> p x e", e=66)
                    tt(mix_s[:, n % 2, :].rearrange("p (x e) -> p x e", e=HD), v6[:, :, 0:HD],
                       comb[:, 6, :].unsqueeze(2).to_broadcast([P, 6, HD]), ALU.mult).then_inc(bc_done, 1)

            def conditioning(L, i):
                part = ADA_PARTS[i]
                dve.wait_ge(ld_bias, 16 * (2 * L + i + 1))
                for a in range(part["nj"] * KT_D):
                    k, j = divmod(a, part["nj"])
                    n = part["a0"] + a
                    dve.wait_ge(ada_full[n % NADA], 16 * (L * NA_TILES // NADA + n // NADA + 1))
                    if k:
                        dve.wait_ge(ada_used, L * NA_TILES + n - part["nj"] + 1)
                    cs = slice(j * ADAW, (j + 1) * ADAW)
                    stt(ada_acc[:, cs], ada_raw[:, n % NADA, :], cond[:, k:k + 1], ada_acc[:, cs], ALU.mult, ALU.add)\
                        .then_inc(ada_used, 1)

            def affine(i, bank):
                ch.tick(V.tensor_copy(aff_b[:, i, :], bank[:, 0:KT_D]))
                ch.tick(stt(aff_a[:, i, :], bank[:, KT_D:2 * KT_D], 1.0, nw_col[:, i, :], ALU.add, ALU.mult))

            def residual(L, which):
                root(L, 2 * which + 1)
                for s in range(NS):
                    ch.link(stt(yn[:, s, :], yn[:, s, :], stat[:, 5, s:s + 1], g_b[:, which, :], ALU.mult, ALU.mult))
                    dve.wait_ge(x_ld[s], 16 * (3 * L + 3 + which))
                    tt(xn[:, s, :], xn[:, s, :], yn[:, s, :], ALU.add).then_inc(x_new, 1)

            for s in range(NS):
                dve.wait_ge(x_ld[s], 16)
                V.memset(stat[:, 0, s:s + 1], 0.0).then_inc(x_new, 1)

            for st in plan.stages:
                for t in {id(o): o for k, o in st["steps"] if k == "M"}.values():
                    for c_ in t["chunks"]:
                        c_["tpar"] = t["ord"] % 2

            with dve.Fori(0, DEPTH) as L:
                ch.loop(L, DVE_STEPS)
                V.memset(ada_acc[:, 0:2 * D], 0.0).then_inc(ada_zero, 1)
                root(L, 0)
                dve.wait_ge(x_st, L * (16 * 2 * NS) + 16)
                scale_rows(L)
                conditioning(L, 0)
                dve.wait_ge(ada_sums, 2 * L + 1)
                dve.wait_ge(ld_par, 16 * 9 * (L + 1))
                affine(0, PS[7])
                ts(sink_b[:, 1, :], sink_b[:, 0, :], 1.0 / SCALE, None, ALU.mult).then_inc(ada_done, 1)
                turned(L, 0)
                ch.link(V.memset(part[:, :, :, :], FLOOR))
                for st in plan.stages:
                    for d in st["dists"]:
                        rope(L, d)
                        if d["width"] == 332:
                            dve.wait_ge(gate_e, L + 1)
                            ch.link(ts(gates[:, :, :], gates[:, :, :], 1.0, None, ALU.add))
                            ch.link(V.reciprocal(gates[:, :, :], gates[:, :, :]))
                        dist(L, st, d)
                    if st["kind"] == "A":
                        dve.wait_ge(v_split, L * NVS + 1)
                        dve.wait_ge(tr_act, L * NJ + d["jobs"][-1]["ord"] + 1)
                        full = cv_T[:, :]
                        win = bass.AP(cv_T, 0, [list(full.ap[0]), [1, CMP_L], [16, N_CMP]])
                        tt(x_blk[:, :, :], win, pe_col[:, :].unsqueeze(2).to_broadcast([P, CMP_L, N_CMP]), ALU.add)\
                            .then_inc(blocks, 1)
                        dve.wait_ge(cmp_act, L + 1)
                        ch.tick(tt(kc_hl[HD:P, 0:N_CMP], PS[4][0:HD, 0:N_CMP], f32(kc_hl[0:HD, 0:N_CMP]), ALU.subtract))
                        tt(vc_lo[0:N_CMP, 0:HD], PS[5][0:N_CMP, 0:HD], f32(vc_hi[0:N_CMP, 0:HD]), ALU.subtract)\
                            .then_inc(cmp_dve, 1)
                    for kind, o in st["steps"]:
                        step(L, st, kind, o)
                combine(L)
                V.memset(ada_acc[:, :], 0.0).then_inc(ada_zero, 1)
                turned(L, 1)
                conditioning(L, 1)
                dve.wait_ge(ada_sums, 2 * L + 2)
                dve.wait_ge(ld_nw, 32 * (L + 1))
                affine(1, PS[0])
                for x in range(4):
                    i, hs = x // 2, slice(x % 2 * HALF, (x % 2 + 1) * HALF)
                    ins = tt(g_b[:, i, hs], PS[1 + x][:, :], g_b[:, i, hs], ALU.mult)
                    if x < 3:
                        ch.tick(ins)
                ins.then_inc(ada_done, 1)
                residual(L, 0)
                root(L, 2)
                dve.wait_ge(x_st, L * (16 * 2 * NS) + 16 * NS + 16)
                scale_rows(L)
                turned(L, 2)
                ch.link(V.memset(gs[:, :, 0:2], 0.0))

                def gate(g):
                    for j in range(2):
                        f = 2 * g + j
                        dve.wait_ge(conv_s, (L * G + g) * 2 + j + 1)
                        ch.link(stt(ct[:, j, :], gs[:, j, 0:S], cw[:, 0, f:f + 1], ct[:, j, :], ALU.mult, ALU.add))
                        stt(ct[:, j, :], gs[:, j, 1:S + 1], cw[:, 1, f:f + 1], ct[:, j, :], ALU.mult, ALU.add)\
                            .then_inc(conv_d, 1)
                    for j in range(2):
                        dve.wait_ge(gelu_s, (L * G + g) * 2 + j + 1)
                        tt(ct[:, j, :], ct[:, j, :], us[:, j, :], ALU.mult).then_inc(gate_d, 1)
                    for j in range(2):
                        dve.wait_ge(act_h, (L * G + g) * 2 + j + 1)
                        tt(a_lo[:, g % 2, j, :], ct[:, j, :], f32(a_hi[:, g % 2, j, :]), ALU.subtract).then_inc(act_l, 1)

                def down(g):
                    for n, p in enumerate(plan.dn[g]):
                        for b in range(8):
                            dve.wait_ge(bank_full, L * NBANK + 8 * p["ord"] + b + 1)
                            dst = yn[:, b, n * HALF:(n + 1) * HALF]
                            if g == 0:
                                V.tensor_copy(dst, PS[b][:, :]).then_inc(evac_v, 1)
                            else:
                                tt(dst, dst, PS[b][:, :], ALU.add).then_inc(evac_v, 1)

                gate(0)
                for g in range(G):
                    down(g)
                    if g + 1 < G:
                        gate(g + 1)
                residual(L, 1)
                ch.close()


_INS = ['x', 'c', 'positions', 'w_in', 'w_out', 'w_ada', 'b_ada', 'norm_w', 'cmp_w_k', 'cmp_w_v', 'cmp_pe_k', 'cmp_pe_v',
        'sinks', 'w_gate', 'w_up', 'conv_w', 'conv_b', 'w_down']


def kernel(**inputs):
    import numpy as np
    import concourse.bacc as bacc
    from concourse.bass_utils import run_bass_kernel_spmd

    nc = bacc.Bacc("TRN2", target_bir_lowering=False, num_devices=1)
    arrays, args = {}, []
    for name in _INS:
        a = np.ascontiguousarray(inputs[name])
        arrays[f"in_{name}"] = a
        args.append(nc.dram_tensor(f"in_{name}", a.shape, mybir.dt.from_np(a.dtype), kind="ExternalInput").ap())
    args.append(nc.dram_tensor("out_0", (1, S, D), F32, kind="ExternalOutput").ap())
    trunk(nc, *args)
    r = run_bass_kernel_spmd(nc, [arrays], core_ids=[0])
    return r.results[0]["out_0"]
```

```python
from contextlib import ExitStack

import concourse.bass as bass
from concourse import mybir

F32 = mybir.dt.float32
F32R = mybir.dt.float32r
BF16 = mybir.dt.bfloat16
I32 = mybir.dt.int32
ALU = mybir.AluOpType
ACT = mybir.ActivationFunctionType
AX = mybir.AxisListType

P = 128
D = 1024
S = 1024
DEPTH = 2
HD = 64
FF = 2816
KT_D = D // P
NS = S // P
HALF = 512
NH = S // HALF
FT = FF // P
N_CMP = S // 16 - 1
CMP_L = 32
NEG = -1e30
FLOOR = -1e28
TINY = 1e-30
EPS = 1e-6
SCALE = HD ** -0.5
THETA = 10000.0
WIN_TILES = 512 // P
MROW = 64

A_Q, A_KC, A_VC, A_KS, A_VS, A_KW, A_VW, A_G = 0, 256, 320, 384, 448, 512, 576, 640
B_Q, B_K, B_V = 652, 1036, 1420
C_Q, C_K, C_V = 1804, 2188, 2316

STAGES = [
    dict(kind="A", passes=[[(A_Q, 320)], [(A_VC, 332)]]),
    dict(kind="C", kv=0, passes=[[(C_Q, 192), (C_K, 64), (C_V, 64)]]),
    dict(kind="C", kv=1, passes=[[(C_Q + 192, 192), (C_K + 64, 64), (C_V + 64, 64)]]),
    dict(kind="B", kv=0, passes=[[(B_Q, 128), (B_K, 128), (B_V, 128)]]),
    dict(kind="B", kv=1, passes=[[(B_Q + 128, 128), (B_K + 128, 128), (B_V + 128, 128)]]),
    dict(kind="B", kv=2, passes=[[(B_Q + 256, 128), (B_K + 256, 128), (B_V + 256, 128)]]),
]
LAYOUTS = {
    "A0": dict(rope=(0, 5, 64), jobs=[(0, "Q", 0), (64, "Q", 1), (128, "Q", 2), (192, "Q", 3), (256, "KC", 0)],
               values=[]),
    "A1": dict(rope=(64, 2, 128), jobs=[(0, "VC", 0), (64, "K", 0), (192, "K", 1)],
               values=[(128, 0), (256, 1)]),
    "C": dict(rope=(0, 4, 64), jobs=[(0, "Q", 0), (64, "Q", 1), (128, "Q", 2), (192, "K", 0)], values=[(256, 0)]),
    "B": dict(rope=(0, 4, 64), jobs=[(0, "Q", 2), (64, "Q", 3), (128, "K", 0), (192, "K", 1)],
              values=[(256, 0), (320, 1)]),
}
BQ = 2


POOL_STEPS, ACT_STEPS, DVE_STEPS = 386, 75, 395

def spread(n, most):
    k = -(-n // most)
    return [n // k + (i < n % k) for i in range(k)]


def chunk_list(tiles, masks, lhs, kv):
    out, at = [], 0
    for n in spread(len(tiles), 4):
        ts = tiles[at:at + n]
        at += n
        out.append(dict(lhs=lhs, kv=kv, key0=ts[0] * P, cols=n * P,
                        masks=[(masks[t], (t - ts[0]) * P) for t in ts if t in masks]))
    return out


def tasks_of(stage):
    kind = stage["kind"]
    out = []
    if kind == "A":
        for i in range(NS):
            cols = []
            win = list(range(max(0, i - WIN_TILES), i + 1))
            for br in range(3):
                for h in range(4):
                    lhs = (h, i * P)
                    if br == 0:
                        cols.append([dict(lhs=lhs, kv="cmp", key0=0, cols=P, masks=[(("cmpS", i), 0)])])
                    elif br == 1:
                        cols.append(chunk_list(list(range(i + 1)), {i: "C"}, lhs, 0))
                    else:
                        m = {i: "C"}
                        if i >= WIN_TILES:
                            m[i - WIN_TILES] = "E"
                        cols.append(chunk_list(win, m, lhs, 1))
            grp = lambda: [dict(q=(0, 4), q0=i * P, n=P, out=0)]
            subs = [dict(br=0, units=[dict(kv="cmp", key=0, groups=grp(), mask=("cmpT", i))]),
                    dict(br=1, units=[dict(kv=0, key=t, groups=grp(), mask="CT" if t == i else None)
                                      for t in range(i + 1)]),
                    dict(br=2, units=[dict(kv=1, key=t, groups=grp(),
                                           mask="CT" if t == i else ("ET" if t == i - WIN_TILES else None))
                                      for t in win])]
            out.append(dict(i=i, lanes=4, cols=cols, subs=subs, rows=12))
    elif kind == "C":
        for i in range(NS):
            ts = list(range(max(0, i - 1), i + 1))
            m = {i: "C", i - 1: "E"}
            cols = [chunk_list(ts, m, (h, i * P), 0) for h in range(3)]
            units = [dict(kv=0, key=t, groups=[dict(q=(0, 3), q0=i * P, n=P, out=0)],
                          mask="CT" if t == i else "ET") for t in ts]
            out.append(dict(i=i, lanes=3, cols=cols, subs=[dict(br=0, units=units)], rows=3))
    else:
        for g in range(NS // 2):
            cols = []
            for h in range(2):
                for b in range(2):
                    blk = 2 * g + b
                    if stage["kv"] == 2:
                        ts, m = [blk], {blk: "B"}
                    else:
                        first = max(0, blk - 1) if stage["kv"] == 0 else max(2 * g, blk - 1)
                        ts = list(range(first, blk + 1))
                        m = {blk: "C", blk - 1: "F"}
                    cols.append(chunk_list(ts, m, (BQ + h, blk * P), h))
            grp = lambda: [dict(q=(BQ + h, 1), q0=2 * g * P, n=2 * P, out=h * 2 * P, kv=h) for h in range(2)]
            if stage["kv"] == 2:
                units = [dict(key=2 * g, mask="BT|"), dict(key=2 * g + 1, mask="|BT")]
            else:
                units = [dict(key=2 * g, mask="CT|FT"), dict(key=2 * g + 1, mask="|CT")]
                if stage["kv"] == 0 and g > 0:
                    units = [dict(key=2 * g - 1, mask="FT|")] + units
            for u in units:
                u["kv"] = None
                u["groups"] = grp()
            out.append(dict(i=g, lanes=4, cols=cols, subs=[dict(br=0, units=units)], rows=4))
    return out


LAG = 2
EARLY = 2


def steps_of(stage, n):
    tasks = tasks_of(stage)
    for t in tasks:
        t["ord"] = n["task"]
        n["task"] += 1
        t["chunks"] = []
        for r, col in enumerate(t["cols"]):
            for j, c in enumerate(col):
                c.update(ord=n["chunk"], row=r, j=j)
                n["chunk"] += 1
                t["chunks"].append(c)
        for s in t["subs"]:
            s.update(ord=n["sub"], task=t)
            n["sub"] += 1
            for k, u in enumerate(s["units"]):
                u.update(ord=n["unit"], sub=s, first=k == 0, last=k == len(s["units"]) - 1, task=t)
                n["unit"] += 1
    units = [u for t in tasks for s in t["subs"] for u in s["units"]]
    at_unit = [[] for _ in units]
    steps, start = [], 0
    for t in tasks:
        first = units.index(t["subs"][0]["units"][0])
        end = first - EARLY
        if end <= 0:
            steps += [("S", c) for c in t["chunks"]] + [("M", t)]
        else:
            room = range(max(start, 0), end)
            many, k = spread(len(t["chunks"]), -(-len(t["chunks"]) // len(room))), 0
            many = [0] * (len(room) - len(many)) + many
            for x, m in zip(room, many):
                at_unit[x] += [("S", c) for c in t["chunks"][k:k + m]]
                k += m
            at_unit[end - 1].append(("M", t))
        start = end
        if first <= 1:
            steps.append(("MT", t))
        else:
            at_unit[first - 2].append(("MT", t))
    waiting_pv, waiting_t = [], []

    def pv(u):
        steps.append(("PV", u))
        for w in waiting_t:
            steps.append(("T", w))
        waiting_t.clear()
        if u["last"]:
            waiting_t.append(u["sub"])

    for u, more in zip(units, at_unit):
        steps.append(("ST", u))
        if waiting_pv:
            steps.append(("R", waiting_pv[-1]))
        steps += more
        waiting_pv.append(u)
        if len(waiting_pv) > LAG:
            pv(waiting_pv.pop(0))
    steps.append(("R", waiting_pv[-1]))
    for u in waiting_pv:
        pv(u)
    for w in waiting_t:
        steps.append(("T", w))
    return steps


TURNS = [(k, h) for k in (0, 1, 5, 6, 7) for h in range(NH)] + [(k, h) for k in (2, 3, 4) for h in range(NH)]
MIX_ORDER = [("C", 0), ("C", 1), ("C", 2)] + [e for i in range(5) for e in (("J", 2 * i), ("C", 3 + i), ("J", 2 * i + 1))] \
    + [("J", j) for j in range(10, 16)]


class Plan:

    def __init__(self):
        n = dict(chunk=0, task=0, unit=0, sub=0)
        self.stages = []
        job = 0
        pn = 0
        for st in STAGES:
            s = dict(st)
            s["unit0"] = n["unit"]
            s["sub0"] = n["sub"]
            s["steps"] = steps_of(st, n)
            s["unit1"] = n["unit"]
            s["sub1"] = n["sub"]
            s["dists"] = []
            for k, cols in enumerate(st["passes"]):
                lay = LAYOUTS[st["kind"] + (str(k) if st["kind"] == "A" else "")]
                jobs = [dict(col=c, what=w, slot=sl, half=h, ord=job + 2 * x + h)
                        for x, (c, w, sl) in enumerate(lay["jobs"]) for h in range(NH)]
                job += len(jobs)
                s["dists"].append(dict(cols=cols, width=sum(c for _, c in cols), lay=lay, jobs=jobs, ord=pn))
                pn += 1
            self.stages.append(s)
        self.n, self.jobs, self.proj = n, job, pn
        for s, nxt in zip(self.stages, self.stages[1:]):
            s["next"], nxt["prev"] = nxt, s
            behind = [x for x, (kind, _) in enumerate(s["steps"]) if kind == "ST"]
            for t in reversed(range(NS)):
                n = (2 * t + 1) * len(behind) // (2 * NS) + 1
                s["steps"].insert(behind[n] if n < len(behind) else len(s["steps"]), ("X", (nxt["dists"][0], t)))
        self.tiles = []
        self.passes = []
        for s in self.stages:
            for d in s["dists"]:
                d["pass"] = self.add("in", [("w_in", k, d["cols"]) for k in range(KT_D)], d["width"])
        self.out_pass = [self.add("out", [("w_out", k, [(n * HALF, HALF)]) for k in range(KT_D)], HALF)
                         for n in range(NH)]
        self.gu, self.dn = {}, {}
        G = FT // 2
        self.gu[0] = self.add("gu", [("gu", k, 0) for k in range(KT_D)], HALF)
        for g in range(G):
            if g + 1 < G:
                self.gu[g + 1] = self.add("gu", [("gu", k, g + 1) for k in range(KT_D)], HALF)
            self.dn[g] = [self.add("dn", [("w_down", 2 * g + j, [(n * HALF, HALF)]) for j in range(2)], HALF)
                          for n in range(NH)]
        self.G = G

    def add(self, kind, tiles, width):
        p = dict(kind=kind, w0=len(self.tiles), n=len(tiles), width=width, ord=len(self.passes))
        self.tiles += [dict(spec=t, width=width, p=p) for t in tiles]
        self.passes.append(p)
        return p


def trunk(nc, x, c, positions, w_in, w_out, w_ada, b_ada, norm_w, cmp_w_k, cmp_w_v, cmp_pe_k, cmp_pe_v,
          sinks, w_gate, w_up, conv_w, conv_b, w_down, out):
    plan = Plan()
    G = plan.G
    mix_dram = nc.dram_tensor("mix_rows", (S, D), F32).ap()
    v_dram = nc.dram_tensor("value_rows", (S, P), F32).ap()
    out2 = out[0]
    x2 = x[0]

    with ExitStack() as ctx:
        def sb(name, shape, dt=F32, where=ctx):
            return where.enter_context(nc.sbuf_tensor(name, shape, dt))

        def sem(name):
            return ctx.enter_context(nc.semaphore(name))

        hT_hi = sb("hT_hi", [P, KT_D, S], F32R)
        hT_lo = sb("hT_lo", [P, KT_D, S], F32R)
        NRAW, NW = 4, 3
        w_raw = sb("w_raw", [P, NRAW, HALF])
        w_hi = sb("w_hi", [P, NW, HALF], F32R)
        w_lo = sb("w_lo", [P, NW, HALF], F32R)
        ident = sb("ident", [P, P])
        ident_b = sb("ident_b", [P, P], BF16)
        strip_T = sb("strip_T", [P, 4, P], BF16)
        strip_BT = sb("strip_BT", [P, 3, P], BF16)
        edge_T = sb("edge_T", [P, P], BF16)
        cmp_T = sb("cmp_T", [P, S], BF16)
        fc_S = sb("fc_S", [P, 2, P], BF16)
        e_S = sb("e_S", [P, P], BF16)
        b_S = sb("b_S", [P, P], BF16)
        CMP_OFF = 8 * (NS - 1)
        cmp_S = sb("cmp_S", [P, CMP_OFF + P], BF16)
        lane_mask = sb("lane_mask", [12, 4, P], BF16)
        row_ones = sb("row_ones", [12, 3])
        sel_m = sb("sel_m", [MROW + 4, 66], F32R)
        ones = sb("ones", [P, P])
        cos_t = sb("cos_t", [P, NS, 32])
        sin_t = sb("sin_t", [P, NS, 32])
        cond = sb("cond", [P, KT_D])
        nw_col = sb("nw_col", [P, 2, KT_D])
        aff_a = sb("aff_a", [P, 2, KT_D])
        aff_b = sb("aff_b", [P, 2, KT_D])
        stat = sb("stat", [P, 7, NS])
        gates = sb("gates", [P, NS, 12])
        sink_b = sb("sink_b", [P, 2, 6])
        pe_col = sb("pe_col", [P, CMP_L])
        cw = sb("cw", [P, 3, FT])
        cb = sb("cb", [P, FT])

        at = ExitStack()
        over_q = ExitStack()
        u_T0 = sb("u_T0", [66, 2, S], F32, over_q)
        sb("u_gap", [66, 2, S], F32, over_q)
        u_T1 = sb("u_T1", [66, 2, S], F32, over_q)
        over_q.close()
        q_hh = sb("q_hh", [P, 4, S], F32R, at)
        q_lm = sb("q_lm", [MROW + 12, 4, S], F32R, at)
        k_hl = sb("k_hl", [P, 2, S], F32R, at)
        k_ho = sb("k_ho", [MROW + 12, 2, S], F32R, at)
        v_hi = sb("v_hi", [P, 2, NS, 66], F32R, at)
        v_lo = sb("v_lo", [P, 2, NS, 66], F32R, at)
        over_pn = ExitStack()
        x_blk = sb("x_blk", [P, CMP_L, N_CMP], F32, over_pn)
        over_pn.close()
        pn = sb("pn", [P, NS, 384], F32, at)
        kc_hl = sb("kc_hl", [P, P], F32R, at)
        kc_ho = sb("kc_ho", [MROW + 12, P], F32R, at)
        vc_hi = sb("vc_hi", [P, 66], F32R, at)
        vc_lo = sb("vc_lo", [P, 66], F32R, at)
        over_p = ExitStack()
        pn_g = sb("pn_g", [P, NS, 332], F32, over_p)
        over_p.close()
        p_f = sb("p_f", [P, 2, HALF], F32, at)
        p_hi = sb("p_hi", [P, 3, HALF], F32R, at)
        p_lo = sb("p_lo", [P, 3, HALF], F32R, at)
        o_T = sb("o_T", [66, 2, HALF], F32, at)
        mix_s = sb("mix_s", [P, 2, 384], F32, at)
        part = sb("part", [P, 2, 12, 2], F32, at)
        m_raw = sb("m_raw", [P, 2, 12], F32, at)
        m_neg = sb("m_neg", [P, 2, 12], F32R, at)
        fin = sb("fin", [P, 2, 3, 4], F32, at)
        fin_t = sb("fin_t", [P, 4, HD], F32, at)
        es = sb("es", [P, 8, 2, 3], F32, at)
        comb = sb("comb", [P, 8, 6], F32, at)
        rope_t = sb("rope_t", [P, 2, 320], F32, at)
        cmpx = ExitStack()
        cv_T = sb("cv_T", [P, S], F32, cmpx)
        w_cmp = sb("w_cmp", [P, CMP_L, HD], F32, cmpx)
        cmpx.close()
        u_T2 = sb("u_T2", [66, 2, S], F32, cmpx)
        v_perm = sb("v_perm", [P, NS, P], F32, cmpx)
        cmpx.close()
        at.close()
        u_T = [u_T0, u_T1, u_T2]
        nat = ExitStack()
        xn = sb("xn", [P, NS, D], F32, nat)
        yn = sb("yn", [P, NS, D], F32, nat)
        junk = sb("junk", [P, D], F32, nat)
        lo_t = sb("lo_t", [P, 2, HALF], F32, nat)
        ada_acc = sb("ada_acc", [P, 4 * D], F32, nat)
        sb("past_ff", [P, 8], F32, nat)
        g_b = sb("g_b", [P, 2, D], F32, nat)
        NADA, ADAW = 4, D
        over_raw = ExitStack()
        sb("two_slots", [P, 2, ADAW], F32, over_raw)
        ada_next = sb("ada_next", [P, 2 * D], F32, over_raw)
        over_raw.close()
        ada_raw = sb("ada_raw", [P, NADA, ADAW], F32, nat)
        nat.close()
        ada = ExitStack()
        sb("xn_place", [P, NS, D], F32, ada)
        ang = sb("ang", [P, 4, NS * 32], F32, ada)
        pos_i = sb("pos_i", [P, NS], I32, ada)
        pos_f = sb("pos_f", [P, NS], F32, ada)
        inv_f = sb("inv_f", [P, 32], F32, ada)
        cc = sb("cc", [P, 3, KT_D], F32, ada)
        ada_raw0 = sb("ada_raw0", [P, NADA, ADAW], F32, ada)
        ada.close()
        ff = ExitStack()
        a_hi = sb("a_hi", [P, 2, 2, S], F32R, ff)
        a_lo = sb("a_lo", [P, 2, 2, S], F32R, ff)
        sb("yn_place", [P, NS, D], F32, ff)
        gs = sb("gs", [P, 2, S + 2], F32, ff)
        us = sb("us", [P, 2, S], F32, ff)
        ct = sb("ct", [P, 2, S], F32, ff)
        ff.close()
        PS = [ctx.enter_context(nc.psum_tensor(f"bank{i}", [P, HALF], F32)) for i in range(8)]

        MASKS = {"C": fc_S[:, 1, :], "F": fc_S[:, 0, :], "E": e_S[:, :], "B": b_S[:, :]}
        MASKS_T = {"CT": strip_T[:, 1, :], "ET": edge_T[:, :],
                   "CT|FT": strip_T[:, 1:3, :], "|CT": strip_T[:, 0:2, :], "FT|": strip_T[:, 2:4, :],
                   "BT|": strip_BT[:, 1:3, :], "|BT": strip_BT[:, 0:2, :]}

        def f32(ap):
            return ap.bitcast(F32)

        NWT = len(plan.tiles)
        raw_at, tot = [], [0] * NRAW
        for w, t in enumerate(plan.tiles):
            nd = 2 if t["spec"][0] == "gu" else len(t["spec"][2])
            tot[w % NRAW] += 16 * nd
            raw_at.append(tot[w % NRAW])
        used_at, used = [], 0
        for t in plan.tiles:
            last = t is plan.tiles[t["p"]["w0"] + t["p"]["n"] - 1]
            used += not last
            used_at.append(None if last else used)
        NBANK = 8 * len(plan.passes)
        ev_a = ev_v = 0
        for p in plan.passes:
            p["a0"], p["v0"] = ev_a, ev_v
            if p["kind"] == "dn":
                ev_v += 8
            else:
                ev_a += 8
        NEV_A, NEV_V = ev_a, ev_v
        NU, NC_, NT_, NSUB = plan.n["unit"], plan.n["chunk"], plan.n["task"], plan.n["sub"]
        NJ = plan.jobs
        dist_list = [(st, d) for st in plan.stages for d in st["dists"]]
        dtr = 0
        vsp = 0
        for st, d in dist_list:
            for j in d["jobs"]:
                dtr += j["what"] in "QK"
                j["dve_after"] = dtr
            vsp += bool(d["lay"]["values"])
            d["v_after"] = vsp
        NDTR, NVS = dtr, vsp
        t_no = 0
        mixn = 0
        for st in plan.stages:
            for kind, o in st["steps"]:
                if kind == "T" and st["kind"] != "B":
                    o["t_no"] = t_no
                    t_no += 1
                    if st["kind"] == "C" or o["br"] == 2:
                        o["mix_no"] = mixn
                        mixn += 1
        NTF, NMIX = t_no, mixn
        es_no = 0
        for st in plan.stages:
            if st["kind"] == "C":
                for kind, o in st["steps"]:
                    if kind == "M":
                        o["es_no"] = es_no
                        es_no += 1
        NES = es_no
        NTT = 3 * 2 * KT_D
        NA_NORM, NA_REST = 2 * KT_D, 4 * KT_D
        NA_TILES = NA_NORM + NA_REST

        ld_c = sem("ld_c")
        ld_par = sem("ld_par")
        ld_norm = sem("ld_norm")
        ld_bias = sem("ld_bias")
        ada_full = [sem(f"ada_full{i}") for i in range(NADA)]
        ada_full0 = [sem(f"ada_full0_{i}") for i in range(NADA)]
        ada_used = sem("ada_used")
        ada_zero = sem("ada_zero")
        ada_sums = sem("ada_sums")
        ada_done = sem("ada_done")
        ld_cmp = sem("ld_cmp")
        ld_nw = sem("ld_nw")
        w_full = [sem(f"w_full{i}") for i in range(NRAW)]
        w_split = sem("w_split")
        w_used = sem("w_used")
        bank_full = sem("bank_full")
        evac_a = sem("evac_a")
        evac_v = sem("evac_v")
        consts = sem("consts")
        attn_init = sem("attn_init")
        x_ld = [sem(f"x_ld{i}") for i in range(NS)]
        mix_ld = [sem(f"mix_ld{i}") for i in range(NS)]
        squared = sem("squared")
        gated = sem("gated")
        squares = sem("squares")
        var_ready = sem("var_ready")
        root_ready = sem("root_ready")
        scaled = sem("scaled")
        scaled_a = sem("scaled_a")
        inverse = sem("inverse")
        tt_full = sem("tt_full")
        tt_act = sem("tt_act")
        tt_dve = sem("tt_dve")
        tt_pool = sem("tt_pool")
        x_new = sem("x_new")
        x_st = sem("x_st")
        roped = sem("roped")
        roped_g = sem("roped_g")
        tr_full = sem("tr_full")
        tr_act = sem("tr_act")
        tr_dve = sem("tr_dve")
        v_split = sem("v_split")
        v_out = sem("v_out")
        v_back = sem("v_back")
        gate_e = sem("gate_e")
        blocks = sem("blocks")
        cmp_full = sem("cmp_full")
        cmp_act = sem("cmp_act")
        cmp_dve = sem("cmp_dve")
        s_full = sem("s_full")
        s_max = sem("s_max")
        m_ready = sem("m_ready")
        mt_full = sem("mt_full")
        m_rows = sem("m_rows")
        st_full = sem("st_full")
        p_exp = sem("p_exp")
        p_rest = sem("p_rest")
        p_rest_g = sem("p_rest_g")
        pv_done = sem("pv_done")
        o_out = sem("o_out")
        t_full = sem("t_full")
        t_done = sem("t_done")
        sink_d = sem("sink_d")
        sink_e = sem("sink_e")
        bc_full = sem("bc_full")
        bc_d = sem("bc_d")
        bc_e = sem("bc_e")
        bc_done = sem("bc_done")
        mix_st = [sem(f"mix_st{i}") for i in range(2)]
        conv_s = sem("conv_s")
        conv_d = sem("conv_d")
        gelu_s = sem("gelu_s")
        gate_d = sem("gate_d")
        act_h = sem("act_h")
        act_l = sem("act_l")
        act_c = sem("act_c")
        dve_c = sem("dve_c")
        pool_c = sem("pool_c")
        rope_tab = sem("rope_tab")
        rope_sin = sem("rope_sin")
        cond_e = sem("cond_e")

        class Chain:

            def __init__(self, eng, s):
                self.eng, self.s, self.n = eng, s, 0
                self.base = 0

            def loop(self, L, each):
                self.base, self.n, self.each = L * each + self.n, 0, each

            def close(self):
                assert self.n == self.each, self.n

            def tick(self, ins):
                ins.then_inc(self.s, 1)
                self.n += 1

            def sync(self):
                self.eng.wait_ge(self.s, self.base + self.n)

            def link(self, ins):
                self.tick(ins)
                self.sync()

        for st, d in dist_list:
            d["pn"] = pn_g if d["width"] == 332 else pn

        def turn_of(site, j):
            return (TURNS[j], PS[j % 6]) if site == 1 else (divmod(j, 2), PS[j % 8])

        SCALED_BY_ACT = (2, 3, 6)
        N_GATED = 3

        def lowered(L, site, j):
            mine = sum(by_pool(site, i) for i in range(j + 1))
            before = [(sum(not by_pool(t, i) for t in range(m) for i in range(16)),
                       sum(by_pool(t, i) for t in range(m) for i in range(16))) for m in (site, 3)]
            return L * before[1][0] + before[0][0] + j + 1 - mine, L * before[1][1] + before[0][1] + mine

        def by_pool(site, j):
            return site != 1 and j % 3 == 1

        def wait_lowered(eng, L, site, j):
            of_dve, of_pool = lowered(L, site, j)
            eng.wait_ge(tt_dve, of_dve)
            if site or j:
                eng.wait_ge(tt_pool, of_pool)

        def rope_views(d, s):
            c0, R, stride = d["lay"]["rope"]
            if stride == HD:
                v = d["pn"][:, s, c0:c0 + R * stride].rearrange("p (r e) -> p r e", e=stride)
            else:
                v = d["pn"][:, s, c0:c0 + 2 * stride].rearrange("p (r e) -> p r e", e=stride)[:, :, 0:HD]
            v = v.rearrange("p r (t i) -> p r t i", t=2)
            t1 = rope_t[:, 0, 0:R * HD].rearrange("p (r t i) -> p r t i", t=2, i=32)
            t2 = rope_t[:, 1, 0:R * HD].rearrange("p (r t i) -> p r t i", t=2, i=32)
            cs = cos_t[:, s, :].unsqueeze(1).unsqueeze(1).to_broadcast([P, R, 2, 32])
            sn = sin_t[:, s, :].unsqueeze(1).to_broadcast([P, R, 32])
            return v, t1, t2, cs, sn

        def rope_count(L, d, s):
            if d["ord"] < 2:
                return roped, (L * 2 + d["ord"]) * NS + s + 1
            return roped_g, (L * (plan.proj - 2) + d["ord"] - 2) * NS + s + 1

        def rest_share(w):
            return w // 2 // 64 * 64

        block = ctx.enter_context(nc.Block())

        def perm(ap, kv, s):
            if kv == 0:
                return ap[:, s * P:(s + 1) * P]
            dil = 4 if kv == 1 else 16
            n = P // dil
            return ap.rearrange("p (c n) -> p n c", c=dil)[:, s * n:(s + 1) * n, :]

        @block.sync
        def _(sp):
            sp.dma_start(cond[:, :], c[0].rearrange("(k p) -> p k", p=P), allow_slow_non_contiguous=True).then_inc(ld_c, 16)
            sp.dma_start(pos_i[:, :], positions[0].rearrange("(s p) -> p s", p=P), allow_slow_non_contiguous=True).then_inc(ld_c, 16)

            def weight(L, w):
                t = plan.tiles[w]
                spec = t["spec"]
                if w >= NRAW:
                    sp.wait_ge(w_split, L * NWT + w - NRAW + 1)
                    sp.nop(nofuse=True)
                slot = w_raw[:, w % NRAW, :]
                full = w_full[w % NRAW]
                if spec[0] == "gu":
                    _, k, g = spec
                    for m, wt in enumerate((w_gate, w_up)):
                        sp.dma_start(slot[:, m * 2 * P:(m + 1) * 2 * P],
                                     wt[L, k * P:(k + 1) * P, g * 2 * P:(g + 1) * 2 * P]).then_inc(full, 16)
                else:
                    name, k, cols = spec
                    wt = {"w_in": w_in, "w_out": w_out, "w_down": w_down}[name]
                    at_ = 0
                    for c0, n in cols:
                        sp.dma_start(slot[:, at_:at_ + n], wt[L, k * P:(k + 1) * P, c0:c0 + n]).then_inc(full, 16)
                        at_ += n

            def mix_store(L, n, i, c0, width):
                sp.dma_start(mix_dram[i * P:(i + 1) * P, c0:c0 + width], mix_s[:, n % 2, 0:width])\
                  .then_inc(mix_st[n % 2], 16)

            def ada_rest(L, a):
                k, j = divmod(a, 4)
                if a >= NADA:
                    sp.wait_ge(ada_used, NA_NORM + L * NA_TILES + a - NADA + 1)
                    sp.nop(nofuse=True)
                c0 = (2 + j) * ADAW
                sp.dma_start(ada_raw[:, a % NADA, :], w_ada[L, k * P:(k + 1) * P, c0:c0 + ADAW])\
                  .then_inc(ada_full[a % NADA], 16)

            def ada_ahead(L, a):
                k, j = divmod(a, 2)
                sp.wait_ge(ada_used, NA_NORM + L * NA_TILES + NA_REST + max(0, a - 1))
                sp.nop(nofuse=True)
                sp.dma_start(ada_raw[:, a % 2, :], w_ada[(L + 1) % DEPTH, k * P:(k + 1) * P, j * ADAW:(j + 1) * ADAW])\
                  .then_inc(ada_full[a % 2], 16)

            for s in range(NS):
                sp.dma_start(xn[:, s, :], x2[s * P:(s + 1) * P, :]).then_inc(x_ld[s], 16)
            sp.wait_ge(ada_zero, 1)
            sp.dma_start(ada_next[0:1, :], b_ada[0:1, 0:2 * D]).then_inc(ld_bias, 16)
            for a in range(NA_NORM):
                k, j = divmod(a, 2)
                if a >= NADA:
                    sp.wait_ge(ada_used, a - NADA + 1)
                sp.dma_start(ada_raw0[:, a % NADA, :], w_ada[0, k * P:(k + 1) * P, j * ADAW:(j + 1) * ADAW])\
                  .then_inc(ada_full0[a % NADA], 16)
            def norm_columns(l):
                for i in range(2):
                    sp.dma_start(nw_col[:, i, :], norm_w[l, 2 * i].rearrange("(k p) -> p k", p=P),
                                 allow_slow_non_contiguous=True).then_inc(ld_norm, 16)

            norm_columns(0)
            sp.wait_ge(ada_used, NA_NORM - NADA)
            for s in range(NS):
                sp.dma_start(out2[s * P:(s + 1) * P, :], xn[:, s, :]).then_inc(x_st, 16)

            with sp.Fori(0, DEPTH) as L:
                par = [(sink_b[:, 0, :], sinks[bass.ts(L, 1), :].to_broadcast([P, 6])),
                       (pe_col[0:HD, :], cmp_pe_k[L].rearrange("l d -> d l")),
                       (pe_col[HD:P, :], cmp_pe_v[L].rearrange("l d -> d l")),
                       (cb[:, :], conv_b[L].rearrange("(t p) -> p t", p=P))]
                par += [(cw[:, i, :], conv_w[L, i].rearrange("(t p) -> p t", p=P)) for i in range(3)]
                for o_, i_ in par:
                    sp.dma_start(o_, i_, allow_slow_non_contiguous=True).then_inc(ld_par, 16)
                wn = 0
                for _ in range(NRAW):
                    weight(L, wn)
                    wn += 1
                sp.wait_ge(ada_done, 3 * L + 1)
                sp.nop(nofuse=True)
                for o_, i_ in ((w_cmp[0:HD, :, :], cmp_w_k[L].rearrange("l d e -> d l e")),
                               (w_cmp[HD:P, :, :], cmp_w_v[L].rearrange("l d e -> d l e"))):
                    sp.dma_start(o_, i_, allow_slow_non_contiguous=True).then_inc(ld_cmp, 16)
                for st in plan.stages:
                    nxt = st.get("next")
                    if nxt:
                        end = nxt["dists"][-1]["pass"]["w0"] + nxt["dists"][-1]["pass"]["n"] + NRAW
                        while wn < end:
                            weight(L, wn)
                            wn += 1
                    if nxt and nxt["kind"] == "B" and nxt["kv"]:
                        p = nxt["dists"][0]["pass"]
                        for s in range(NS):
                            sp.wait_ge(evac_a, L * NEV_A + p["a0"] + s + 1)
                            sp.nop(nofuse=True)
                            sp.dma_start(v_dram[s * P:(s + 1) * P, :], pn[:, s, 256:384]).then_inc(v_out, 16)
                        sp.wait_ge(v_out, 16 * NS * (L * 2 + nxt["kv"]))
                        sp.nop(nofuse=True)
                        sp.wait_ge(v_split, L * NVS + nxt["dists"][0]["v_after"] - 1)
                        sp.nop(nofuse=True)
                        for i in range(NS):
                            if nxt["kv"] == 1:
                                v = v_dram.rearrange("(n c) d -> c n d", c=4)
                                sp.dma_start(v_perm[:, i, :], v[i // 2, (i % 2) * P:(i % 2 + 1) * P, :]).then_inc(v_back, 8 * 2)
                            else:
                                v = v_dram.rearrange("(n c) d -> c n d", c=16)
                                for b in range(2):
                                    sp.dma_start(v_perm[b * 64:(b + 1) * 64, i, :], v[2 * i + b]).then_inc(v_back, 16)
                    if st["kind"] != "B":
                        for kind, o in st["steps"]:
                            if kind == "T" and "mix_no" in o:
                                sp.wait_ge(t_done, L * NTF + o["t_no"] + 1)
                                sp.nop(nofuse=True)
                                c0, width = (0, 256) if st["kind"] == "A" else (640 + 192 * st["kv"], 192)
                                mix_store(L, o["mix_no"], o["task"]["i"], c0, width)
                for i in range(2):
                    sp.wait_ge(mix_st[i], (L + 1) * (16 * NMIX // 2))
                    sp.nop(nofuse=True)
                sp.wait_ge(pv_done, (L + 1) * NU)
                sp.nop(nofuse=True)
                for s in range(NS):
                    for cs in (slice(0, 256), slice(640, D)):
                        sp.dma_start(yn[:, s, cs], mix_dram[s * P:(s + 1) * P, cs]).then_inc(mix_ld[s], 16)
                sp.wait_ge(ada_zero, 2 * L + 2)
                sp.nop(nofuse=True)
                sp.dma_start(ada_acc[0:1, :], b_ada[bass.ts(L, 1), 2 * D:6 * D]).then_inc(ld_bias, 16)
                for i in range(2):
                    sp.dma_start(g_b[:, i, :], norm_w[bass.ts(L, 1), 1 + 2 * i, :].to_broadcast([P, D])).then_inc(ld_nw, 16)
                a = 0
                while wn < plan.out_pass[1]["w0"] + KT_D or a < 4 * KT_D:
                    for _ in range(3):
                        if a < 4 * KT_D:
                            ada_rest(L, a)
                            a += 1
                    if wn < plan.out_pass[1]["w0"] + KT_D:
                        weight(L, wn)
                        wn += 1
                for s in range(NS):
                    sp.dma_start(xn[:, s, :], out2[s * P:(s + 1) * P, :]).then_inc(x_ld[s], 16)
                for _ in range(NRAW):
                    weight(L, wn)
                    wn += 1
                for s in range(NS):
                    sp.wait_ge(x_new, (2 * L + 1) * NS + s + 1)
                    sp.nop(nofuse=True)
                    sp.dma_start(out2[s * P:(s + 1) * P, :], xn[:, s, :]).then_inc(x_st, 16)
                sp.wait_ge(ada_done, 3 * L + 3)
                sp.nop(nofuse=True)
                norm_columns((L + 1) % DEPTH)
                sp.wait_ge(ada_zero, 2 * L + 3)
                sp.nop(nofuse=True)
                sp.dma_start(ada_next[0:1, :], b_ada[bass.ts((L + 1) % DEPTH, 1), 0:2 * D]).then_inc(ld_bias, 16)
                for g in range(G):
                    if 1 <= g <= KT_D:
                        ada_ahead(L, 2 * g - 2)
                        ada_ahead(L, 2 * g - 1)
                    while wn < min(NWT, plan.dn[g][1]["w0"] + 2 + NRAW):
                        weight(L, wn)
                        wn += 1
                sp.wait_ge(x_st, 16 * NS * (2 * L + 2))
                sp.nop(nofuse=True)
                sp.wait_ge(bank_full, (L + 1) * NBANK)
                sp.nop(nofuse=True)
                for s in range(NS):
                    sp.dma_start(xn[:, s, :], out2[s * P:(s + 1) * P, :]).then_inc(x_ld[s], 16)
                for s in range(NS):
                    sp.wait_ge(x_new, (2 * L + 2) * NS + s + 1)
                    sp.nop(nofuse=True)
                    sp.dma_start(out2[s * P:(s + 1) * P, :], xn[:, s, :]).then_inc(x_st, 16)
            sp.wait_ge(x_st, 16 * NS * (2 * DEPTH + 1))

        @block.gpsimd
        def _(pool):
            ch = Chain(pool, pool_c)
            for m in (ident, ident_b):
                ch.link(nc.gpsimd.memset(m[:, :], 0.0))
                ch.tick(nc.gpsimd.affine_select(out=m[:, :], in_=m[:, :], compare_op=ALU.not_equal, fill=1.0, base=0,
                                                pattern=[[-1, P]], channel_multiplier=1))
            ch.tick(nc.gpsimd.memset(ones[:, :], 1.0))
            for m in (strip_T, strip_BT):
                ch.tick(nc.gpsimd.memset(m[:, :, :], NEG))
            zero = [strip_T[:, 1, :], strip_T[:, 2, :], strip_BT[:, 1, :], edge_T[:, :], cmp_T[:, :], fc_S[:, 0, :],
                    fc_S[:, 1, :], e_S[:, :], b_S[:, :], cmp_S[:, :], lane_mask[:, :, :]]
            ch.sync()
            for m in zero:
                ch.tick(nc.gpsimd.memset(m, 0.0))
            ch.tick(nc.gpsimd.memset(row_ones[:, :], 1.0))
            ch.tick(nc.gpsimd.memset(f32(sel_m[:, :]), 0.0))
            ch.sync()

            def keep(m, cmp, base, cm, pattern, fill=NEG):
                ch.tick(nc.gpsimd.affine_select(out=m, in_=m, compare_op=cmp, fill=fill, base=base, pattern=pattern,
                                                channel_multiplier=cm))

            one = [[1, P]]
            neg = [[-1, P]]
            keep(strip_T[:, 1, :], ALU.is_ge, 0, -1, one)
            keep(strip_T[:, 2, :], ALU.is_ge, 0, 1, neg)
            keep(edge_T[:, :], ALU.is_gt, 0, 1, neg)
            keep(strip_BT[:, 1, :], ALU.is_ge, 0, -1, one)
            keep(cmp_T[:, :], ALU.is_ge, -(CMP_L - 1), -16, [[1, S]])
            keep(fc_S[:, 0, :], ALU.is_ge, 0, -1, one)
            keep(fc_S[:, 1, :], ALU.is_ge, 0, 1, neg)
            keep(e_S[:, :], ALU.is_gt, 0, -1, one)
            keep(b_S[:, :], ALU.is_ge, 0, 1, neg)
            keep(cmp_S[:, :], ALU.is_ge, 16 * CMP_OFF - (CMP_L - 1), 1, [[-16, CMP_OFF + P]])
            keep(row_ones[:, :], ALU.is_ge, 0, 1, [[-4, 3]], 0.0)
            ch.sync()
            keep(strip_BT[:, 1, 64:P], ALU.is_ge, -64, 1, [[0, 64]])
            keep(b_S[:, 0:64], ALU.is_ge, 63, -1, [[0, 64]])
            keep(row_ones[:, :], ALU.is_ge, 3, -1, [[4, 3]], 0.0)
            for br in range(3):
                keep(lane_mask[:, :, :], ALU.not_equal, -4 * br, 1, [[-1, 4], [0, P]], 1.0)
                ch.sync()
            nc.gpsimd.memset(f32(sel_m[MROW:MROW + 4, 65:66]), -1.0).then_inc(consts, 1)
            pool.wait_ge(consts, 1)

            def rope(L, d, s):
                tt = nc.gpsimd.tensor_tensor
                pool.wait_ge(evac_a, L * NEV_A + d["pass"]["a0"] + s + 1)
                pool.nop(nofuse=True)
                v, t1, t2, cs, sn = rope_views(d, s)
                ch.tick(tt(t1, v, cs, ALU.mult))
                ch.tick(tt(t2[:, :, 0, :], v[:, :, 1, :], sn, ALU.mult))
                ch.tick(tt(t2[:, :, 1, :], v[:, :, 0, :], sn, ALU.mult))
                ch.sync()
                ch.tick(tt(v[:, :, 0, :], t1[:, :, 0, :], t2[:, :, 0, :], ALU.subtract))
                tt(v[:, :, 1, :], t1[:, :, 1, :], t2[:, :, 1, :], ALU.add).then_inc(roped_g, 1)
                pool.wait_ge(*rope_count(L, d, s))

            def lower_parts(L, st):
                if "prev" not in st:
                    pool.wait_ge(roped, (L + 1) * 2 * NS)
                    pool.nop(nofuse=True)
                for kind, o in st["steps"]:
                    if kind == "X":
                        rope(L, *o)
                    if kind == "R":
                        n = L * NU + o["ord"]
                        w = o["task"]["lanes"] * P
                        c0 = w - rest_share(w)
                        pool.wait_ge(p_exp, n + 1)
                        pool.nop(nofuse=True)
                        nc.gpsimd.tensor_tensor(p_lo[:, o["ord"] % 3, c0:w], p_f[:, o["ord"] % 2, c0:w],
                                                f32(p_hi[:, o["ord"] % 3, c0:w]), ALU.subtract).then_inc(p_rest_g, 1)

            def split(L, w):
                t = plan.tiles[w]
                n = t["width"]
                pool.wait_ge(w_full[w % NRAW], L * tot[w % NRAW] + raw_at[w])
                back = w - NW
                if back >= 0:
                    if used_at[back] is not None:
                        pool.wait_ge(w_used, L * used + used_at[back])
                    else:
                        pool.wait_ge(bank_full, L * NBANK + 8 * (plan.tiles[back]["p"]["ord"] + 1))
                pool.nop(nofuse=True)
                src = w_raw[:, w % NRAW, 0:n]
                ch.link(nc.gpsimd.tensor_copy(w_hi[:, w % NW, 0:n], src))
                nc.gpsimd.tensor_tensor(w_lo[:, w % NW, 0:n], src, f32(w_hi[:, w % NW, 0:n]), ALU.subtract)\
                  .then_inc(w_split, 1)

            def turned(L, site, j):
                k, h = divmod(j, 2)
                hs = slice(h * HALF, (h + 1) * HALF)
                pool.wait_ge(tt_act, (L * 3 + site) * 16 + j + 1)
                pool.nop(nofuse=True)
                nc.gpsimd.tensor_tensor(hT_lo[:, k, hs], lo_t[:, 1, :], f32(hT_hi[:, k, hs]), ALU.subtract)\
                  .then_inc(tt_pool, 1)

            def gate_rows(L, which):
                if which == 0:
                    pool.wait_ge(ada_done, 3 * L + 2)
                    pool.nop(nofuse=True)
                for s in range(N_GATED):
                    pool.wait_ge(squared, (2 * L + which) * NS + s + 1)
                    pool.nop(nofuse=True)
                    nc.gpsimd.tensor_tensor(yn[:, s, :], yn[:, s, :], g_b[:, which, :], ALU.mult).then_inc(gated, 1)

            with pool.Fori(0, DEPTH) as L:
                ch.loop(L, POOL_STEPS)
                for j, w in ((1, None), (4, 0), (7, 1), (10, None), (13, 2)):
                    turned(L, 0, j)
                    if w is not None:
                        split(L, w)
                wait_lowered(pool, L, 0, 15)
                pool.nop(nofuse=True)
                for m, val in ((v_hi[:, :, :, 64:65], 1.0), (v_hi[:, :, :, 65:66], 0.0), (v_lo[:, :, :, 64:66], 0.0),
                               (kc_hl[:, :], 0.0), (kc_ho[:, :], 0.0), (vc_hi[:, 0:64], 0.0), (vc_hi[:, 64:65], 1.0),
                               (vc_hi[:, 65:66], 0.0)):
                    ch.tick(nc.gpsimd.memset(f32(m), val))
                nc.gpsimd.memset(f32(vc_lo[:, :]), 0.0).then_inc(attn_init, 1)
                w = NW
                for st, d in dist_list:
                    while w < d["pass"]["w0"] + d["pass"]["n"] :
                        split(L, w)
                        w += 1
                    if "prev" in st:
                        lower_parts(L, st["prev"])
                    if "next" in st:
                        for _ in range(NW):
                            split(L, w)
                            w += 1
                    if d["lay"]["values"]:
                        if st["kind"] == "B" and st["kv"]:
                            k = NS if st["kv"] == 1 else 3 * NS
                            pool.wait_ge(v_back, 16 * (L * 3 * NS + k))
                            src = v_perm[:, :, :]
                            off = 256
                        else:
                            src, off = d["pn"][:, :, :], 0
                        pool.wait_ge(evac_a, L * NEV_A + d["pass"]["a0"] + 8)
                        if "prev" in st:
                            pool.wait_ge(pv_done, L * NU + st["unit0"])
                        pool.nop(nofuse=True)
                        for c0, slot in d["lay"]["values"]:
                            ch.tick(nc.gpsimd.tensor_copy(v_hi[:, slot, :, 0:HD], src[:, :, c0 - off:c0 - off + HD]))
                        ch.sync()
                        vs = d["lay"]["values"]
                        for c0, slot in vs:
                            ins = nc.gpsimd.tensor_tensor(v_lo[:, slot, :, 0:HD], src[:, :, c0 - off:c0 - off + HD],
                                                          f32(v_hi[:, slot, :, 0:HD]), ALU.subtract)
                            if slot == vs[-1][1]:
                                ins.then_inc(v_split, 1)
                            else:
                                ch.tick(ins)
                lower_parts(L, plan.stages[-1])
                while w < plan.gu[0]["w0"] + NW:
                    split(L, w)
                    w += 1
                gate_rows(L, 0)
                for j in range(16):
                    if by_pool(2, j):
                        turned(L, 2, j)
                while w < NWT:
                    split(L, w)
                    w += 1
                gate_rows(L, 1)
                ch.close()

        @block.tensor
        def _(pe):
            mm = nc.tensor.matmul
            pe.wait_ge(consts, 1)

            def turned_out(L, site, b):
                j = [j for j in range(16) if turn_of(site, j)[1] is PS[b]]
                if j:
                    pe.wait_ge(tt_act, (L * 3 + site) * 16 + j[-1] + 1)
                    wait_lowered(pe, L, site, j[-1])

            def run_pass(L, p, bufs=0, after=None, site=None):
                kind = p["kind"]
                for k in range(p["n"]):
                    w = p["w0"] + k
                    pe.wait_ge(w_split, L * NWT + w + 1)
                    hi, lo = w_hi[:, w % NW, :], w_lo[:, w % NW, :]
                    for b in range(8):
                        if k == 0:
                            bank_free(L, p, b)
                            if site is not None:
                                turned_out(L, site, b)
                            if after is not None:
                                stage_freed(L, after, b)
                        first, last = k == 0, k == p["n"] - 1
                        if kind == "gu":
                            j, m, h = b // 4, b // 2 % 2, b % 2
                            cs = slice(m * 2 * P + j * P, m * 2 * P + (j + 1) * P)
                            rs = slice(h * HALF, (h + 1) * HALF)
                            prods = [(hi[:, cs], hT_hi[:, k, rs]), (hi[:, cs], hT_lo[:, k, rs]),
                                     (lo[:, cs], hT_hi[:, k, rs])]
                            o_ = PS[b][:, :]
                        else:
                            a, al = (a_hi[:, bufs, k], a_lo[:, bufs, k]) if kind == "dn" else (hT_hi[:, k], hT_lo[:, k])
                            qs = slice(b * P, (b + 1) * P)
                            n = p["width"]
                            prods = [(a[:, qs], hi[:, 0:n]), (a[:, qs], lo[:, 0:n]), (al[:, qs], hi[:, 0:n])]
                            o_ = PS[b][:, 0:n]
                        for x, (l_, r_) in enumerate(prods):
                            ins = mm(o_, l_, r_, start=first and x == 0, stop=last and x == 2)
                        if last:
                            ins.then_inc(bank_full, 1)
                    if not last:
                        ins.then_inc(w_used, 1)

            def stage_freed(L, st, b):
                jobs = st["dists"][-1]["jobs"]
                if b < 4:
                    old = [j for x, j in enumerate(jobs) if x % 4 == b][-1]
                    pe.wait_ge(tr_act, L * NJ + old["ord"] + 1)
                    pe.wait_ge(tr_dve, L * NDTR + old["dve_after"])
                elif b == 4 and st["kind"] == "A":
                    pe.wait_ge(cmp_dve, L + 1)
                elif b == 4:
                    attention_over(L, st["prev"])

            def bank_free(L, p, b):
                prev = plan.passes[p["ord"] - 1] if p["ord"] else None
                if prev is not None and prev["kind"] == "dn":
                    pe.wait_ge(evac_v, L * NEV_V + prev["v0"] + b + 1)
                elif prev is not None:
                    pe.wait_ge(evac_a, L * NEV_A + prev["a0"] + b + 1)

            def columns(L, bank, sums, j0):
                for x in range(2 * KT_D):
                    ins = mm(bank[:, x:x + 1], sums[:, j0 + x * P:j0 + (x + 1) * P], ones[:, 0:1], start=True, stop=True)
                return ins

            def turned(L, site):
                for j in range(16):
                    if site == 0 and j == 7:
                        pe.wait_ge(ada_done, 3 * L + 1)
                    turn(L, site, j)

            def turn(L, site, j):
                (k, h), bank = turn_of(site, j)
                n = (L * 3 + site) * 16 + j
                back = 6 if site == 1 else 8
                if j >= back:
                    pe.wait_ge(tt_act, n - back + 1)
                    wait_lowered(pe, L, site, j - back)
                for t in range(4):
                    s = 4 * h + t
                    if site != 1 and k == 0:
                        mine = sum(t in SCALED_BY_ACT for t in range(s + 1))
                        if s in SCALED_BY_ACT:
                            pe.wait_ge(scaled_a, (2 * L + (site == 2)) * len(SCALED_BY_ACT) + mine)
                        else:
                            pe.wait_ge(scaled, (2 * L + (site == 2)) * (NS - len(SCALED_BY_ACT)) + s + 1 - mine)
                    elif site == 1 and k == 0:
                        pe.wait_ge(mix_ld[s], 32 * (L + 1))
                    elif site == 1 and k == 2:
                        pe.wait_ge(bc_done, L * NS + s + 1)
                    ins = mm(bank[:, t * P:(t + 1) * P], yn[:, s, k * P:(k + 1) * P], ident[:, :],
                             start=True, stop=True, is_transpose=True)
                ins.then_inc(tt_full, 1)

            def dist(L, st, d):
                base = L * NJ
                turned_tiles = set()
                for j in d["jobs"]:
                    n = j["ord"]
                    if j is d["jobs"][0]:
                        pe.wait_ge(evac_a, L * NEV_A + st["dists"][-1]["pass"]["a0"] + 4)
                    x = d["jobs"].index(j)
                    if x >= 4:
                        old = d["jobs"][x - 4]
                        pe.wait_ge(tr_act, base + old["ord"] + 1)
                        pe.wait_ge(tr_dve, L * NDTR + old["dve_after"])
                    for t in range(4):
                        s = 4 * j["half"] + t
                        if j["what"] in ("Q", "K", "KC"):
                            if s not in turned_tiles:
                                pe.wait_ge(*rope_count(L, d, s))
                                turned_tiles.add(s)
                        else:
                            pe.wait_ge(evac_a, L * NEV_A + d["pass"]["a0"] + s + 1)
                        pe.nop(nofuse=True)
                        src = d["pn"][:, s, j["col"]:j["col"] + HD]
                        if j["what"] == "Q":
                            mm(PS[x % 4][HD:P, t * P:(t + 1) * P], src, ident[:, :], start=True, stop=True)
                        ins = mm(PS[x % 4][0:HD, t * P:(t + 1) * P], src, ident[:, :], start=True, stop=True,
                                 is_transpose=True)
                    ins.then_inc(tr_full, 1)

            def compress(L):
                pe.wait_ge(blocks, L + 1)
                pe.wait_ge(ld_cmp, 32 * (L + 1))
                pe.nop(nofuse=True)
                for l_ in range(CMP_L):
                    mm(PS[4][0:HD, 0:N_CMP], w_cmp[0:HD, l_, :], x_blk[0:HD, l_, :], start=l_ == 0, stop=l_ == CMP_L - 1)
                for l_ in range(CMP_L):
                    ins = mm(PS[5][0:N_CMP, 0:HD], x_blk[HD:P, l_, :], w_cmp[HD:P, l_, :],
                             start=l_ == 0, stop=l_ == CMP_L - 1)
                ins.then_inc(cmp_full, 1)

            def step(L, st, kind, o):
                if kind == "S":
                    n = L * NC_ + o["ord"]
                    if o["ord"] >= 2:
                        pe.wait_ge(s_max, n - 1)
                    slot, q0 = o["lhs"]
                    keys = kc_hl[:, :] if o["kv"] == "cmp" else k_hl[:, o["kv"], o["key0"]:o["key0"] + o["cols"]]
                    bank = PS[o["ord"] % 2]
                    ins = mm(bank[:, 0:o["cols"]], q_hh[:, slot, q0:q0 + P], keys, start=True, stop=not o["masks"],
                             skip_group_check=True)
                    for x, (m, off) in enumerate(o["masks"]):
                        if isinstance(m, tuple):
                            a = CMP_OFF - 8 * m[1]
                            src = cmp_S[:, a:a + P]
                        else:
                            src = MASKS[m]
                        ins = mm(bank[:, off:off + P], ident_b[:, :], src, start=False,
                                 stop=x == len(o["masks"]) - 1, skip_group_check=True)
                    ins.then_inc(s_full, 1)
                elif kind == "MT":
                    n = L * NT_ + o["ord"]
                    pe.wait_ge(m_ready, n + 1)
                    if o["ord"]:
                        pe.wait_ge(m_rows, n)
                    mm(PS[7][0:o["rows"], 0:P], f32(m_neg[:, o["ord"] % 2, 0:o["rows"]]), ident[:, :],
                       start=True, stop=True, is_transpose=True).then_inc(mt_full, 1)
                elif kind == "ST":
                    n = L * NU + o["ord"]
                    if o["ord"] >= 2:
                        pe.wait_ge(p_exp, n - 1)
                    if o["sub"]["units"][0] is o:
                        pe.wait_ge(m_rows, L * NT_ + o["task"]["ord"] + 1)
                    bank = PS[2 + o["ord"] % 2]
                    K2 = MROW + o["task"]["rows"]
                    gs_ = o["groups"]
                    first = True
                    for g_ in gs_:
                        kv = g_.get("kv", o["kv"])
                        q0, nq = g_["q"]
                        w = nq * g_["n"]
                        ks = slice(o["key"] * P, (o["key"] + 1) * P)
                        k1, k2 = (kc_hl[:, :], kc_ho[0:K2, :]) if kv == "cmp" else (k_hl[:, kv, ks], k_ho[0:K2, kv, ks])
                        cs = slice(g_["q0"], g_["q0"] + g_["n"])
                        o_ = bank[:, g_["out"]:g_["out"] + w]
                        mm(o_, k1, q_hh[:, q0:q0 + nq, cs], start=first, stop=False, skip_group_check=True)
                        first = False
                        ins = mm(o_, k2, q_lm[0:K2, q0:q0 + nq, cs], start=False,
                                 stop=g_ is gs_[-1] and o["mask"] is None, skip_group_check=True)
                    if o["mask"] is not None:
                        m = o["mask"]
                        if isinstance(m, tuple):
                            src = cmp_T[:, m[1] * P:(m[1] + 1) * P].unsqueeze(1).to_broadcast([P, 4, P])
                        elif "|" in m:
                            src = MASKS_T[m].unsqueeze(1).to_broadcast([P, 2, 2, P])
                        else:
                            src = MASKS_T[m].unsqueeze(1).to_broadcast([P, o["task"]["lanes"], P])
                        ins = mm(bank[:, 0:o["task"]["lanes"] * P], ident_b[:, :], src, start=False, stop=True,
                                 skip_group_check=True)
                    ins.then_inc(st_full, 1)
                elif kind == "PV":
                    n = L * NU + o["ord"]
                    s = o["sub"]
                    pe.wait_ge(p_rest, n + 1)
                    pe.wait_ge(p_rest_g, n + 1)
                    bank = PS[4 + s["ord"] % 2]
                    if o["first"] and s["ord"] >= 2:
                        pe.wait_ge(o_out, L * NSUB + s["ord"] - 1)
                    ph, pl = p_hi[:, o["ord"] % 3, :], p_lo[:, o["ord"] % 3, :]
                    gs_ = o["groups"]
                    start = o["first"]
                    for g_ in gs_:
                        kv = g_.get("kv", o["kv"])
                        w = g_["q"][1] * g_["n"]
                        cs = slice(g_["out"], g_["out"] + w)
                        vh, vl = (vc_hi[:, :], vc_lo[:, :]) if kv == "cmp" else (v_hi[:, kv, o["key"], :], v_lo[:, kv, o["key"], :])
                        for x, (l_, r_) in enumerate(((vh, ph), (vh, pl), (vl, ph))):
                            stop = o["last"] and g_ is gs_[-1] and x == 2 and st["kind"] != "B"
                            ins = mm(bank[0:66, cs], l_, r_[:, cs], start=start, stop=stop, skip_group_check=True)
                            start = False
                    ins.then_inc(pv_done, 1)
                    if o["last"] and st["kind"] == "B":
                        g0 = o["task"]["i"] * 2 * P
                        for g_ in gs_:
                            cs = slice(g_["out"], g_["out"] + 2 * P)
                            ins = mm(bank[0:66, cs], sel_m[MROW:MROW + 4, :], q_lm[MROW:MROW + 4, g_["q"][0], g0:g0 + 2 * P],
                                     start=False, stop=g_ is gs_[-1], skip_group_check=True)
                        ins.then_inc(cmp_full, 1)
                elif kind == "T" and st["kind"] != "B":
                    n = L * NTF + o["t_no"]
                    pe.wait_ge(o_out, L * NSUB + o["ord"] + 1)
                    if o["t_no"]:
                        pe.wait_ge(t_done, n)
                    for l_ in range(o["task"]["lanes"]):
                        ins = mm(PS[6][:, l_ * 66:(l_ + 1) * 66], o_T[:, o["ord"] % 2, l_ * P:(l_ + 1) * P],
                                 ident[0:66, 0:66], start=True, stop=True, is_transpose=True)
                    ins.then_inc(t_full, 1)

            def combine(L, s):
                if s >= 2:
                    pe.wait_ge(bc_done, L * NS + s - 1)
                for x in range(6):
                    ins = mm(PS[6 + s % 2][:, x * 66:(x + 1) * 66], u_T[x // 2][:, x % 2, s * P:(s + 1) * P],
                             ident[0:66, 0:66], start=True, stop=True, is_transpose=True)
                ins.then_inc(bc_full, 1)

            def scores_read(L, st):
                last = st["steps"]
                pe.wait_ge(s_max, L * NC_ + max(o["ord"] for k, o in last if k == "S") + 1)
                pe.wait_ge(p_exp, L * NU + st["unit1"])

            def attention_over(L, st):
                last = st["steps"]
                pe.wait_ge(m_rows, L * NT_ + max(o["ord"] for k, o in last if k == "M") + 1)
                pe.wait_ge(o_out, L * NSUB + st["sub1"])
                ts = [o["t_no"] for k, o in last if k == "T" and "t_no" in o]
                if ts:
                    pe.wait_ge(t_done, L * NTF + max(ts) + 1)

            with pe.Fori(0, DEPTH) as L:
                pe.wait_ge(x_new, (2 * L + 1) * NS)
                pe.wait_ge(ada_used, NA_NORM + L * NA_TILES)
                columns(L, PS[7], ada_next, 0).then_inc(ada_sums, 1)
                turned(L, 0)
                for d in plan.stages[0]["dists"]:
                    run_pass(L, d["pass"], site=0 if d is plan.stages[0]["dists"][0] else None)
                for st in plan.stages:
                    if "prev" in st:
                        scores_read(L, st["prev"])
                    for d in st["dists"]:
                        dist(L, st, d)
                        last = d["jobs"][-1]
                        if d is not st["dists"][-1]:
                            pe.wait_ge(tr_act, L * NJ + last["ord"] + 1)
                            pe.wait_ge(tr_dve, L * NDTR + last["dve_after"])
                    if st["kind"] == "A":
                        pe.wait_ge(attn_init, L + 1)
                        compress(L)
                    nxt = st.get("next")
                    if nxt:
                        p = nxt["dists"][0]["pass"]
                        run_pass(L, p, after=st)
                        pe.wait_ge(evac_a, L * NEV_A + p["a0"] + 2)
                    else:
                        attention_over(L, st["prev"])
                    pe.wait_ge(tr_act, L * NJ + last["ord"] + 1)
                    pe.wait_ge(tr_dve, L * NDTR + last["dve_after"])
                    pe.wait_ge(v_split, L * NVS + d["v_after"])
                    first_m = [kind for kind, _ in st["steps"]].index("M")
                    for x, (kind, o) in enumerate(st["steps"]):
                        if x == first_m and nxt:
                            pe.wait_ge(evac_a, L * NEV_A + p["a0"] + 8)
                        step(L, st, kind, o)
                scores_read(L, plan.stages[-1])
                attention_over(L, plan.stages[-1])
                for kind, x in MIX_ORDER:
                    if kind == "C":
                        combine(L, x)
                    else:
                        turn(L, 1, x)
                for n, p in enumerate(plan.out_pass):
                    run_pass(L, p, site=None if n else 1)
                pe.wait_ge(evac_a, L * NEV_A + plan.out_pass[1]["a0"] + 5)
                pe.wait_ge(ada_used, NA_NORM + L * NA_TILES + NA_REST)
                for x in range(4):
                    c0 = (0 if x < 2 else 3) * D + x % 2 * HALF
                    ins = mm(PS[x][:, :], ones[:, :], ada_acc[:, c0:c0 + HALF], start=True, stop=True)
                ins.then_inc(ada_sums, 1)
                columns(L, PS[4], ada_acc, D).then_inc(ada_sums, 1)
                pe.wait_ge(ada_done, 3 * L + 3)
                pe.wait_ge(evac_a, L * NEV_A + plan.out_pass[1]["a0"] + 8)
                turned(L, 2)
                run_pass(L, plan.gu[0], site=2)
                for g in range(G):
                    if g + 1 < G:
                        run_pass(L, plan.gu[g + 1])
                    pe.wait_ge(act_l, (L * G + g + 1) * 2)
                    for p in plan.dn[g]:
                        run_pass(L, p, g % 2)

        @block.scalar
        def _(act):
            ch = Chain(act, act_c)
            A = nc.scalar.activation
            act.wait_ge(ld_c, 32)
            A(cc[:, 0, :], cond[:, :], ACT.Exp, scale=-1.0).then_inc(cond_e, 1)
            act.wait_ge(rope_tab, 1)
            A(sin_t[:, :, :].rearrange("p a b -> p (a b)"), ang[:, 1, :], ACT.Sin)
            A(cos_t[:, :, :].rearrange("p a b -> p (a b)"), ang[:, 2, :], ACT.Sin).then_inc(rope_sin, 1)

            def square(src, s, cs, row):
                return A(junk[:, cs], src[:, s, cs], ACT.Square, accum_out=stat[:, row, s:s + 1])

            def root(L, site):
                n = L * 4 + site
                A(junk[:, 0:8], stat[:, 0, :], ACT.Copy).then_inc(squares, 1)
                act.wait_ge(var_ready, n + 1)
                A(stat[:, 2, :], stat[:, 1, :], ACT.Sqrt).then_inc(root_ready, 1)

            def scale_rows(L, site):
                act.wait_ge(inverse, 4 * L + site + 1)
                act.wait_ge(x_new, (2 * L + 1 + site // 2) * NS)
                for s in SCALED_BY_ACT:
                    A(yn[:, s, :], xn[:, s, :], ACT.Identity, scale=stat[:, 5, s:s + 1]).then_inc(scaled_a, 1)

            def new_rows(L, which):
                for s in range(NS):
                    act.wait_ge(x_new, (2 * L + 1 + which) * NS + s + 1)
                    ch.link(square(xn, s, slice(0, D), 0))

            def turned(L, site, js=range(16)):
                for j in js:
                    n = (L * 3 + site) * 16 + j
                    (k, h), bank = turn_of(site, j)
                    act.wait_ge(tt_full, n + 1)
                    o_ = hT_hi[:, k, h * HALF:(h + 1) * HALF]
                    if site == 1:
                        A(o_, bank[:, :], ACT.Copy).then_inc(tt_act, 1)
                    else:
                        i = site // 2
                        ins = A(o_, bank[:, :], ACT.Identity, scale=aff_a[:, i, k:k + 1], bias=aff_b[:, i, k:k + 1])
                        if by_pool(site, j):
                            ch.tick(ins)
                            if j > 1:
                                act.wait_ge(tt_pool, lowered(L, site, j - 1)[1])
                            ins = A(lo_t[:, 1, :], bank[:, :], ACT.Identity, scale=aff_a[:, i, k:k + 1],
                                    bias=aff_b[:, i, k:k + 1])
                        ins.then_inc(tt_act, 1)

            def out_of_banks(L, p, dst):
                for b in range(8):
                    act.wait_ge(bank_full, L * NBANK + 8 * p["ord"] + b + 1)
                    A(dst(b), PS[b][:, 0:p["width"]], ACT.Copy).then_inc(evac_a, 1)

            def dist(L, st, d):
                base = L * NJ
                kvp = st["kv"] if st["kind"] == "B" else 0
                for j in d["jobs"]:
                    bank = PS[d["jobs"].index(j) % 4]
                    act.wait_ge(tr_full, base + j["ord"] + 1)
                    h, sl = j["half"], j["slot"]
                    hs = slice(h * HALF, (h + 1) * HALF)

                    def put(dst, src, fn=ACT.Copy):
                        if kvp == 0:
                            return A(dst[:, hs], src, fn)
                        dil = 4 if kvp == 1 else 16
                        m = HALF // dil
                        dv = dst.rearrange("p (c n) -> p n c", c=dil)[:, h * m:(h + 1) * m, :]
                        return A(dv, src.rearrange("p (n c) -> p n c", c=dil), fn)

                    if j["what"] == "Q":
                        put(q_hh[:, sl, :], bank[:, :]).then_inc(tr_act, 1)
                    elif j["what"] == "K":
                        if h == 0:
                            col = 0 if st["kind"] != "A" else 1 + sl
                            ch.tick(A(k_ho[MROW:MROW + 12, sl, :], row_ones[:, col:col + 1].to_broadcast([12, S]), ACT.Copy))
                        ch.tick(put(k_ho[0:HD, sl, :], bank[0:HD, :]))
                        put(k_hl[0:HD, sl, :], bank[0:HD, :]).then_inc(tr_act, 1)
                    elif j["what"] == "KC":
                        A(cv_T[0:HD, hs], bank[0:HD, :], ACT.Copy).then_inc(tr_act, 1)
                    else:
                        A(cv_T[HD:P, hs], bank[0:HD, :], ACT.Copy).then_inc(tr_act, 1)

            def step(L, st, kind, o):
                if kind == "MT" and st["kind"] == "C":
                    n = L * NES + o["es_no"]
                    act.wait_ge(sink_d, n + 1)
                    A(es[:, o["ord"] % 8, 1, :], es[:, o["ord"] % 8, 0, :], ACT.Exp).then_inc(sink_e, 1)
                elif kind == "ST":
                    n = L * NU + o["ord"]
                    w = o["task"]["lanes"] * P
                    act.wait_ge(st_full, n + 1)
                    bank = PS[2 + o["ord"] % 2]
                    if o["ord"] >= 2:
                        act.wait_ge(p_rest, n - 1)
                        act.wait_ge(p_rest_g, n - 1)
                    A(p_f[:, o["ord"] % 2, 0:w], bank[:, 0:w], ACT.Exp, scale=SCALE)
                    if o["ord"] >= 3:
                        act.wait_ge(pv_done, n - 2)
                    A(p_hi[:, o["ord"] % 3, 0:w], bank[:, 0:w], ACT.Exp, scale=SCALE).then_inc(p_exp, 1)
                elif kind == "PV" and o["last"]:
                    s = o["sub"]
                    n = L * NSUB + s["ord"]
                    bank = PS[4 + s["ord"] % 2]
                    w = o["task"]["lanes"] * P
                    if st["kind"] == "B":
                        act.wait_ge(cmp_full, L * (1 + 12) + 1 + st["kv"] * 4 + o["task"]["i"] + 1)
                        g0 = o["task"]["i"]
                        for h in range(2):
                            dst = u_T[st["kv"]][:, h, :]
                            src = bank[0:66, h * 2 * P:(h + 1) * 2 * P]
                            if st["kv"] == 0:
                                dst = dst[:, g0 * 2 * P:(g0 + 1) * 2 * P]
                            elif st["kv"] == 1:
                                dst = dst.rearrange("p (n c) -> p c n", c=4)[:, g0, :]
                            else:
                                dst = dst.rearrange("p (n c) -> p c n", c=16)[:, 4 * g0:4 * g0 + 4, :]
                                src = src.rearrange("p (c n) -> p c n", c=4)
                            ins = A(dst, src, ACT.Copy)
                        ins.then_inc(o_out, 1)
                    else:
                        act.wait_ge(pv_done, L * NU + o["ord"] + 1)
                        A(o_T[:, s["ord"] % 2, 0:w], bank[0:66, 0:w], ACT.Copy).then_inc(o_out, 1)

            for s in range(NS):
                act.wait_ge(x_new, s + 1)
                ch.link(square(xn, s, slice(0, D), 0))

            with act.Fori(0, DEPTH) as L:
                ch.loop(L, ACT_STEPS)
                root(L, 0)
                scale_rows(L, 0)
                act.wait_ge(ada_done, 3 * L + 1)
                turned(L, 0)
                for d in plan.stages[0]["dists"]:
                    out_of_banks(L, d["pass"], lambda b: d["pn"][:, b, 0:d["width"]])
                act.wait_ge(evac_a, L * NEV_A + d["pass"]["a0"] + 8)
                A(gates[:, :, :], pn_g[:, :, 320:332], ACT.Exp, scale=-1.0).then_inc(gate_e, 1)
                act.wait_ge(x_st, 16 * NS * (2 * L + 1))
                for st in plan.stages:
                    for d in st["dists"]:
                        dist(L, st, d)
                    if st["kind"] == "A":
                        act.wait_ge(cmp_full, L * (1 + 12) + 1)
                        act.wait_ge(attn_init, L + 1)
                        ch.tick(A(kc_ho[MROW:MROW + 12, :], row_ones[:, 0:1].to_broadcast([12, P]), ACT.Copy))
                        ch.tick(A(kc_ho[0:HD, 0:N_CMP], PS[4][0:HD, 0:N_CMP], ACT.Copy))
                        ch.tick(A(kc_hl[0:HD, 0:N_CMP], PS[4][0:HD, 0:N_CMP], ACT.Copy))
                        A(vc_hi[0:N_CMP, 0:HD], PS[5][0:N_CMP, 0:HD], ACT.Copy).then_inc(cmp_act, 1)
                    if "next" in st:
                        nd = st["next"]["dists"][0]
                        if "prev" in st:
                            act.wait_ge(v_split, L * NVS + st["dists"][0]["v_after"])
                        out_of_banks(L, nd["pass"], lambda b: pn[:, b, 0:nd["width"]])
                    for kind, o in st["steps"]:
                        step(L, st, kind, o)
                for kind, x in MIX_ORDER:
                    if kind == "C":
                        act.wait_ge(bc_d, L * NS + x + 1)
                        A(comb[:, 2, :], comb[:, 1, :], ACT.Exp, scale=SCALE).then_inc(bc_e, 1)
                    else:
                        turned(L, 1, [x])
                halves = [slice(0, HALF), slice(HALF, D)]
                out_of_banks(L, plan.out_pass[0], lambda b: yn[:, b, halves[0]])
                act.wait_ge(evac_a, L * NEV_A + plan.out_pass[0]["a0"] + 8)
                for s in range(NS):
                    ch.link(square(yn, s, halves[0], 0))
                for b in range(NS):
                    p = plan.out_pass[1]
                    act.wait_ge(bank_full, L * NBANK + 8 * p["ord"] + b + 1)
                    A(yn[:, b, halves[1]], PS[b][:, :], ACT.Copy).then_inc(evac_a, 1)
                    act.wait_ge(evac_a, L * NEV_A + p["a0"] + b + 1)
                    square(yn, b, halves[1], 6).then_inc(squared, 1)
                    act.wait_ge(squared, 2 * L * NS + b + 1)
                root(L, 1)
                new_rows(L, 0)
                root(L, 2)
                scale_rows(L, 2)
                turned(L, 2)

                act.wait_ge(x_st, 16 * NS * (2 * L + 2))

                def gu(g):
                    if g:
                        act.wait_ge(gate_d, (L * G + g) * 2)
                    out_of_banks(L, plan.gu[g], lambda b: gs[:, b // 4, 2 + b % 2 * HALF:2 + (b % 2 + 1) * HALF]
                                 if b // 2 % 2 == 0 else us[:, b // 4, b % 2 * HALF:(b % 2 + 1) * HALF])
                    act.wait_ge(evac_a, L * NEV_A + plan.gu[g]["a0"] + 8)
                    for j in range(2):
                        f = 2 * g + j
                        if g:
                            act.wait_ge(act_l, (L * G + g - 1) * 2 + j + 1)
                        A(ct[:, j, :], gs[:, j, 2:S + 2], ACT.Identity, scale=cw[:, 2, f:f + 1], bias=cb[:, f:f + 1])\
                            .then_inc(conv_s, 1)
                    for j in range(2):
                        act.wait_ge(conv_d, (L * G + g) * 2 + j + 1)
                        A(ct[:, j, :], ct[:, j, :], ACT.Gelu_apprx_tanh).then_inc(gelu_s, 1)
                    for j in range(2):
                        act.wait_ge(gate_d, (L * G + g) * 2 + j + 1)
                        if g >= 2:
                            act.wait_ge(bank_full, L * NBANK + 8 * (plan.dn[g - 2][1]["ord"] + 1))
                        A(a_hi[:, g % 2, j, :], ct[:, j, :], ACT.Copy).then_inc(act_h, 1)

                for g in range(G):
                    gu(g)
                for n in range(2):
                    for s in range(NS):
                        act.wait_ge(evac_v, L * NEV_V + plan.dn[G - 1][n]["v0"] + s + 1)
                        ins = square(yn, s, halves[n], 6 * n)
                        if n == 0:
                            ch.link(ins)
                        else:
                            ins.then_inc(squared, 1)
                            act.wait_ge(squared, (2 * L + 1) * NS + s + 1)
                root(L, 3)
                new_rows(L, 1)
                ch.close()

        @block.vector
        def _(dve):
            ch = Chain(dve, dve_c)
            V = nc.vector
            tt, ts, stt = V.tensor_tensor, V.tensor_scalar, V.scalar_tensor_tensor
            dve.wait_ge(cond_e, 1)
            ch.link(ts(cc[:, 1, :], cc[:, 0, :], 1.0, None, ALU.add))
            ch.link(V.reciprocal(cc[:, 2, :], cc[:, 1, :]))
            ch.link(tt(cond[:, :], cond[:, :], cc[:, 2, :], ALU.mult))
            import math
            for i in range(32):
                ch.tick(V.memset(inv_f[:, i:i + 1], float(THETA ** (-2.0 * i / HD))))
            dve.wait_ge(ld_c, 32)
            ch.link(V.tensor_copy(pos_f[:, :], pos_i[:, :]))
            a3 = ang[:, 0, :].rearrange("p (s i) -> p s i", i=32)
            ch.link(tt(a3, pos_f[:, :].unsqueeze(2).to_broadcast([P, NS, 32]),
                       inv_f[:, :].unsqueeze(1).to_broadcast([P, NS, 32]), ALU.mult))
            BIG = 1.5 * 2 ** 23
            ch.link(ts(ang[:, 1, :], ang[:, 0, :], 1 / (2 * math.pi), BIG, ALU.mult, ALU.add))
            ch.link(ts(ang[:, 1, :], ang[:, 1, :], -BIG, None, ALU.add))
            c1 = 6.28125
            c2 = 1981 / 2 ** 20 + 0.0
            c3 = 2 * math.pi - c1 - c2
            for cn in (c1, c2, c3):
                ch.link(stt(ang[:, 0, :], ang[:, 1, :], -cn, ang[:, 0, :], ALU.mult, ALU.add))
            pi = 3.1415925
            ch.link(ts(ang[:, 1, :], ang[:, 0, :], pi, -pi, ALU.min, ALU.max))
            ch.link(ts(ang[:, 2, :], ang[:, 1, :], -1.0, None, ALU.mult))
            ch.link(tt(ang[:, 2, :], ang[:, 1, :], ang[:, 2, :], ALU.max))
            ts(ang[:, 2, :], ang[:, 2, :], -1.0, math.pi / 2, ALU.mult, ALU.add).then_inc(rope_tab, 1)
            dve.wait_ge(rope_sin, 1)

            def root(L, site):
                n = L * 4 + site
                dve.wait_ge(squares, n + 1)
                ins = ts(stat[:, 1, :], stat[:, 0, :], 1.0 / D, EPS, ALU.mult, ALU.add)
                if site % 2:
                    ch.link(ins)
                    ins = stt(stat[:, 1, :], stat[:, 6, :], 1.0 / D, stat[:, 1, :], ALU.mult, ALU.add)
                ins.then_inc(var_ready, 1)
                dve.wait_ge(root_ready, n + 1)
                ch.link(V.reciprocal(stat[:, 3, :], stat[:, 2, :]))
                ch.link(tt(stat[:, 4, :], stat[:, 1, :], stat[:, 3, :], ALU.mult))
                ch.link(tt(stat[:, 4, :], stat[:, 4, :], stat[:, 3, :], ALU.mult))
                ch.link(ts(stat[:, 4, :], stat[:, 4, :], -0.5, 1.5, ALU.mult, ALU.add))
                tt(stat[:, 5, :], stat[:, 4, :], stat[:, 3, :], ALU.mult).then_inc(inverse, 1)
                dve.wait_ge(inverse, n + 1)

            def scale_rows(L):
                for s in range(NS):
                    if s not in SCALED_BY_ACT:
                        ts(yn[:, s, :], xn[:, s, :], stat[:, 5, s:s + 1], None, ALU.mult).then_inc(scaled, 1)

            def turned(L, site, js=range(16)):
                for j in js:
                    if by_pool(site, j):
                        continue
                    n = (L * 3 + site) * 16 + j
                    (k, h), bank = turn_of(site, j)
                    hs = slice(h * HALF, (h + 1) * HALF)
                    dve.wait_ge(tt_act, n + 1)
                    src = bank[:, :]
                    if site != 1:
                        i = site // 2
                        if j:
                            dve.wait_ge(tt_dve, lowered(L, site, j - 1)[0])
                        ch.link(ts(lo_t[:, 0, :], src, aff_a[:, i, k:k + 1], aff_b[:, i, k:k + 1], ALU.mult, ALU.add))
                        src = lo_t[:, 0, :]
                    tt(hT_lo[:, k, hs], src, f32(hT_hi[:, k, hs]), ALU.subtract).then_inc(tt_dve, 1)

            def rope(L, d):
                for s in range(NS):
                    dve.wait_ge(evac_a, L * NEV_A + d["pass"]["a0"] + s + 1)
                    v, t1, t2, cs, sn = rope_views(d, s)
                    ch.tick(tt(t1, v, cs, ALU.mult))
                    ch.tick(tt(t2[:, :, 0, :], v[:, :, 1, :], sn, ALU.mult))
                    ch.tick(tt(t2[:, :, 1, :], v[:, :, 0, :], sn, ALU.mult))
                    ch.sync()
                    ch.tick(tt(v[:, :, 0, :], t1[:, :, 0, :], t2[:, :, 0, :], ALU.subtract))
                    tt(v[:, :, 1, :], t1[:, :, 1, :], t2[:, :, 1, :], ALU.add).then_inc(roped, 1)
                    dve.wait_ge(*rope_count(L, d, s))

            def dist(L, st, d):
                kvp = st["kv"] if st["kind"] == "B" else 0
                for j in d["jobs"]:
                    if j["what"] not in "QK":
                        continue
                    bank = PS[d["jobs"].index(j) % 4]
                    h, sl = j["half"], j["slot"]
                    dve.wait_ge(tr_act, L * NJ + j["ord"] + 1)

                    def view(t):
                        if kvp == 0:
                            return t[:, h * HALF:(h + 1) * HALF]
                        dil = 4 if kvp == 1 else 16
                        m = HALF // dil
                        return t.rearrange("p (c n) -> p n c", c=dil)[:, h * m:(h + 1) * m, :]

                    def src(ap):
                        return ap if kvp == 0 else ap.rearrange("p (n c) -> p n c", c=4 if kvp == 1 else 16)

                    if j["what"] == "Q":
                        tt(view(q_lm[0:HD, sl, :]), src(bank[0:HD, :]), f32(view(q_hh[0:HD, sl, :])), ALU.subtract)\
                            .then_inc(tr_dve, 1)
                    else:
                        tt(view(k_hl[HD:P, sl, :]), src(bank[0:HD, :]), f32(view(k_hl[0:HD, sl, :])), ALU.subtract)\
                            .then_inc(tr_dve, 1)

            def mix_free(L, n):
                if n >= 2:
                    dve.wait_ge(mix_st[n % 2], L * (16 * NMIX // 2) + 16 * (n // 2))

            def step(L, st, kind, o):
                if kind == "S":
                    n = L * NC_ + o["ord"]
                    dve.wait_ge(s_full, n + 1)
                    V.tensor_reduce(part[:, o["tpar"], o["row"], o["j"]:o["j"] + 1], PS[o["ord"] % 2][:, 0:o["cols"]],
                                    AX.X, ALU.max).then_inc(s_max, 1)
                elif kind == "M":
                    r, par = o["rows"], o["ord"] % 2
                    dve.wait_ge(s_max, L * NC_ + o["chunks"][-1]["ord"] + 1)
                    ch.link(V.tensor_reduce(m_raw[:, par, 0:r], part[:, par, 0:r, :], AX.X, ALU.max))
                    if st["kind"] == "C":
                        q = 3 * st["kv"]
                        ch.link(tt(m_raw[:, par, 0:3], m_raw[:, par, 0:3], sink_b[:, 1, q:q + 3], ALU.max))
                    ts(m_neg[:, par, 0:r], m_raw[:, par, 0:r], -1.0, None, ALU.mult).then_inc(m_ready, 1)
                    ch.link(V.memset(part[:, par, :, :], FLOOR))
                    if st["kind"] == "C":
                        q = 3 * st["kv"]
                        dve.wait_ge(m_ready, L * NT_ + o["ord"] + 1)
                        stt(es[:, o["ord"] % 8, 0, :], f32(m_neg[:, par, 0:3]), SCALE, sink_b[:, 0, q:q + 3], ALU.mult, ALU.add)\
                            .then_inc(sink_d, 1)
                elif kind == "MT":
                    r = o["rows"]
                    dve.wait_ge(mt_full, L * NT_ + o["ord"] + 1)
                    q0 = o["i"] * P
                    if st["kind"] == "B":
                        q0 = o["i"] * 2 * P
                        dst = q_lm[MROW:MROW + 4, BQ:BQ + 2, q0:q0 + 2 * P].rearrange("p h (b q) -> p h b q", b=2)
                        src = PS[7][0:4, 0:P].unsqueeze(1).unsqueeze(1).to_broadcast([4, 2, 2, P])
                        msk = lane_mask[0:4, :, :].rearrange("p (h b) q -> p h b q", h=2)
                    else:
                        n = o["lanes"]
                        dst = q_lm[MROW:MROW + r, 0:n, q0:q0 + P]
                        src = PS[7][0:r, 0:P].unsqueeze(1).to_broadcast([r, n, P])
                        msk = lane_mask[0:r, 0:n, :]
                    tt(dst, src, msk, ALU.mult).then_inc(m_rows, 1)
                elif kind == "R":
                    n = L * NU + o["ord"]
                    w = o["task"]["lanes"] * P
                    w -= rest_share(w)
                    dve.wait_ge(p_exp, n + 1)
                    tt(p_lo[:, o["ord"] % 3, 0:w], p_f[:, o["ord"] % 2, 0:w], f32(p_hi[:, o["ord"] % 3, 0:w]), ALU.subtract)\
                        .then_inc(p_rest, 1)
                elif kind == "T" and st["kind"] != "B":
                    dve.wait_ge(t_full, L * NTF + o["t_no"] + 1)
                    n = o["task"]["lanes"]
                    v = PS[6][:, 0:n * 66].rearrange("p (h e) -> p h e", e=66)
                    par = o["ord"] % 2
                    i = o["task"]["i"]
                    s_, r_, w_ = fin[:, par, 0, 0:n], fin[:, par, 1, 0:n], fin[:, par, 2, 0:n]
                    sums = v[:, :, 64:65].rearrange("p h e -> p (h e)")
                    if st["kind"] == "A":
                        ch.link(ts(s_, sums, TINY, None, ALU.max))
                        ch.link(V.reciprocal(r_, s_))
                        g_ = gates[:, i, :].rearrange("p (h b) -> p h b", b=3)[:, :, o["br"]]
                        ch.link(tt(w_, r_, g_, ALU.mult))
                        dst = mix_s[:, i % 2, 0:256].rearrange("p (h e) -> p h e", e=HD)
                        wb = w_.unsqueeze(2).to_broadcast([P, n, HD])
                        if o["br"] == 0:
                            mix_free(L, o["task"]["subs"][2]["mix_no"])
                            tt(dst, v[:, :, 0:HD], wb, ALU.mult).then_inc(t_done, 1)
                            dve.wait_ge(t_done, L * NTF + o["t_no"] + 1)
                        else:
                            ch.link(tt(fin_t[:, :, :], v[:, :, 0:HD], wb, ALU.mult))
                            tt(dst, dst, fin_t[:, :, :], ALU.add).then_inc(t_done, 1)
                            dve.wait_ge(t_done, L * NTF + o["t_no"] + 1)
                    else:
                        dve.wait_ge(sink_e, L * NES + o["task"]["es_no"] + 1)
                        ch.link(tt(s_, sums, es[:, o["task"]["ord"] % 8, 1, :], ALU.add))
                        ch.link(V.reciprocal(r_, s_))
                        mix_free(L, o["mix_no"])
                        dst = mix_s[:, o["mix_no"] % 2, 0:192].rearrange("p (h e) -> p h e", e=HD)
                        tt(dst, v[:, :, 0:HD], r_.unsqueeze(2).to_broadcast([P, n, HD]), ALU.mult).then_inc(t_done, 1)

            def combine(L, s):
                dve.wait_ge(bc_full, L * NS + s + 1)
                v = PS[6 + s % 2][:, 0:6 * 66].rearrange("p (g h e) -> p g h e", g=3, h=2)
                m = v[:, :, :, 65]
                l_ = v[:, :, :, 64]
                gh = lambda i: comb[:, i, :].rearrange("p (g h) -> p g h", g=3)
                over_g = lambda i: comb[:, i, :].rearrange("p (g h) -> p h g", g=3)
                ch.link(V.tensor_reduce(comb[:, 0, 0:2], m.rearrange("p g h -> p h g"), AX.X, ALU.max))
                tt(gh(1), m, comb[:, 0, 0:2].unsqueeze(1).to_broadcast([P, 3, 2]), ALU.subtract).then_inc(bc_d, 1)
                dve.wait_ge(bc_e, L * NS + s + 1)
                ch.link(tt(gh(3), gh(2), l_, ALU.mult))
                ch.link(V.tensor_reduce(comb[:, 4, 0:2], over_g(3), AX.X, ALU.add))
                ch.link(V.reciprocal(comb[:, 5, 0:2], comb[:, 4, 0:2]))
                ch.link(tt(gh(6), gh(2), comb[:, 5, 0:2].unsqueeze(1).to_broadcast([P, 3, 2]), ALU.mult))
                v6 = PS[6 + s % 2][:, 0:6 * 66].rearrange("p (x e) -> p x e", e=66)
                tt(yn[:, s, 256:640].rearrange("p (x e) -> p x e", e=HD), v6[:, :, 0:HD],
                   comb[:, 6, :].unsqueeze(2).to_broadcast([P, 6, HD]), ALU.mult).then_inc(bc_done, 1)

            def add_up(full, count, raw, sums, k, j, nj, used):
                dve.wait_ge(full, count)
                if k:
                    dve.wait_ge(ada_used, used - nj + 1)
                cs = slice(j * ADAW, (j + 1) * ADAW)
                stt(sums[:, cs], raw, cond[:, k:k + 1], sums[:, cs], ALU.mult, ALU.add).then_inc(ada_used, 1)

            def ada_rest(L):
                dve.wait_ge(ld_bias, 16 * (2 * L + 2))
                for a in range(NA_REST):
                    m = a % NADA
                    add_up(ada_full[m], 16 * (L * (16 if m < 2 else 8) + a // NADA + 1), ada_raw[:, m, :], ada_acc,
                           a // 4, a % 4, 4, NA_NORM + L * NA_TILES + a)

            def ada_ahead(L, a):
                add_up(ada_full[a % 2], 16 * (L * 16 + 8 + a // 2 + 1), ada_raw[:, a % 2, :], ada_next,
                       a // 2, a % 2, 2, NA_NORM + L * NA_TILES + NA_REST + a)

            def affine(i, bank):
                ch.tick(V.tensor_copy(aff_b[:, i, :], bank[:, 0:KT_D]))
                return stt(aff_a[:, i, :], bank[:, KT_D:2 * KT_D], 1.0, nw_col[:, i, :], ALU.add, ALU.mult)

            def residual(L, which):
                for s in range(N_GATED, NS):
                    dve.wait_ge(squared, (2 * L + which) * NS + s + 1)
                    ch.tick(tt(yn[:, s, :], yn[:, s, :], g_b[:, which, :], ALU.mult))
                root(L, 2 * which + 1)
                for s in range(NS):
                    dve.wait_ge(x_ld[s], 16 * (2 * L + 2 + which))
                    if s < N_GATED:
                        dve.wait_ge(gated, (2 * L + which) * N_GATED + s + 1)
                    stt(xn[:, s, :], yn[:, s, :], stat[:, 5, s:s + 1], xn[:, s, :], ALU.mult, ALU.add).then_inc(x_new, 1)

            V.memset(ada_next[:, :], 0.0).then_inc(ada_zero, 1)
            for s in range(NS):
                dve.wait_ge(x_ld[s], 16)
                V.memset(stat[:, 0, s:s + 1], 0.0).then_inc(x_new, 1)

            for st in plan.stages:
                for t in {id(o): o for k, o in st["steps"] if k == "M"}.values():
                    for c_ in t["chunks"]:
                        c_["tpar"] = t["ord"] % 2

            dve.wait_ge(ld_bias, 16)
            for a in range(NA_NORM):
                add_up(ada_full0[a % NADA], 16 * (a // NADA + 1), ada_raw0[:, a % NADA, :], ada_next, a // 2, a % 2, 2, a)
            dve.wait_ge(ada_used, NA_NORM)

            with dve.Fori(0, DEPTH) as L:
                ch.loop(L, DVE_STEPS)
                root(L, 0)
                scale_rows(L)
                dve.wait_ge(ada_sums, 3 * L + 1)
                dve.wait_ge(ld_norm, 32 * (L + 1))
                affine(0, PS[7]).then_inc(ada_done, 1)
                turned(L, 0)
                dve.wait_ge(ld_par, 16 * 7 * (L + 1))
                ch.link(ts(sink_b[:, 1, :], sink_b[:, 0, :], 1.0 / SCALE, None, ALU.mult))
                ch.link(V.memset(part[:, :, :, :], FLOOR))
                for d in plan.stages[0]["dists"]:
                    rope(L, d)
                for st in plan.stages:
                    for d in st["dists"]:
                        dist(L, st, d)
                    if st["kind"] == "A":
                        dve.wait_ge(gate_e, L + 1)
                        ch.link(ts(gates[:, :, :], gates[:, :, :], 1.0, None, ALU.add))
                        ch.link(V.reciprocal(gates[:, :, :], gates[:, :, :]))
                        dve.wait_ge(tr_act, L * NJ + d["jobs"][-1]["ord"] + 1)
                        full = cv_T[:, :]
                        win = bass.AP(cv_T, 0, [list(full.ap[0]), [1, CMP_L], [16, N_CMP]])
                        tt(x_blk[:, :, :], win, pe_col[:, :].unsqueeze(2).to_broadcast([P, CMP_L, N_CMP]), ALU.add)\
                            .then_inc(blocks, 1)
                        dve.wait_ge(cmp_act, L + 1)
                        ch.tick(tt(kc_hl[HD:P, 0:N_CMP], PS[4][0:HD, 0:N_CMP], f32(kc_hl[0:HD, 0:N_CMP]), ALU.subtract))
                        tt(vc_lo[0:N_CMP, 0:HD], PS[5][0:N_CMP, 0:HD], f32(vc_hi[0:N_CMP, 0:HD]), ALU.subtract)\
                            .then_inc(cmp_dve, 1)
                    for kind, o in st["steps"]:
                        step(L, st, kind, o)
                for kind, x in MIX_ORDER:
                    if kind == "C":
                        combine(L, x)
                    else:
                        turned(L, 1, [x])
                V.memset(ada_acc[:, :], 0.0).then_inc(ada_zero, 1)
                ada_rest(L)
                dve.wait_ge(ada_sums, 3 * L + 2)
                dve.wait_ge(ld_nw, 32 * (L + 1))
                for x in range(4):
                    i, hs = x // 2, slice(x % 2 * HALF, (x % 2 + 1) * HALF)
                    ins = tt(g_b[:, i, hs], PS[x][:, :], g_b[:, i, hs], ALU.mult)
                    if x < 3:
                        ch.tick(ins)
                ins.then_inc(ada_done, 1)
                dve.wait_ge(ada_done, 3 * L + 2)
                residual(L, 0)
                dve.wait_ge(ada_sums, 3 * L + 3)
                affine(1, PS[4]).then_inc(ada_done, 1)
                dve.wait_ge(ada_done, 3 * L + 3)
                root(L, 2)
                scale_rows(L)
                turned(L, 2)
                wait_lowered(dve, L, 2, 15)
                ch.link(V.memset(gs[:, :, 0:2], 0.0))
                V.memset(ada_next[:, :], 0.0).then_inc(ada_zero, 1)
                dve.wait_ge(ld_bias, 16 * (2 * L + 3))

                def gate(g):
                    for j in range(2):
                        f = 2 * g + j
                        dve.wait_ge(conv_s, (L * G + g) * 2 + j + 1)
                        ch.link(stt(ct[:, j, :], gs[:, j, 0:S], cw[:, 0, f:f + 1], ct[:, j, :], ALU.mult, ALU.add))
                        stt(ct[:, j, :], gs[:, j, 1:S + 1], cw[:, 1, f:f + 1], ct[:, j, :], ALU.mult, ALU.add)\
                            .then_inc(conv_d, 1)
                    for j in range(2):
                        dve.wait_ge(gelu_s, (L * G + g) * 2 + j + 1)
                        tt(ct[:, j, :], ct[:, j, :], us[:, j, :], ALU.mult).then_inc(gate_d, 1)
                    for j in range(2):
                        dve.wait_ge(act_h, (L * G + g) * 2 + j + 1)
                        tt(a_lo[:, g % 2, j, :], ct[:, j, :], f32(a_hi[:, g % 2, j, :]), ALU.subtract).then_inc(act_l, 1)

                def down(g):
                    for n, p in enumerate(plan.dn[g]):
                        for b in range(8):
                            dve.wait_ge(bank_full, L * NBANK + 8 * p["ord"] + b + 1)
                            dst = yn[:, b, n * HALF:(n + 1) * HALF]
                            if g == 0:
                                V.tensor_copy(dst, PS[b][:, :]).then_inc(evac_v, 1)
                            else:
                                tt(dst, dst, PS[b][:, :], ALU.add).then_inc(evac_v, 1)

                gate(0)
                for g in range(G):
                    down(g)
                    if g < KT_D:
                        ada_ahead(L, 2 * g)
                        ada_ahead(L, 2 * g + 1)
                    if g + 1 < G:
                        gate(g + 1)
                residual(L, 1)
                ch.close()


_INS = ['x', 'c', 'positions', 'w_in', 'w_out', 'w_ada', 'b_ada', 'norm_w', 'cmp_w_k', 'cmp_w_v', 'cmp_pe_k', 'cmp_pe_v',
        'sinks', 'w_gate', 'w_up', 'conv_w', 'conv_b', 'w_down']


def kernel(**inputs):
    import numpy as np
    import concourse.bacc as bacc
    from concourse.bass_utils import run_bass_kernel_spmd

    nc = bacc.Bacc("TRN2", target_bir_lowering=False, num_devices=1)
    arrays, args = {}, []
    for name in _INS:
        a = np.ascontiguousarray(inputs[name])
        arrays[f"in_{name}"] = a
        args.append(nc.dram_tensor(f"in_{name}", a.shape, mybir.dt.from_np(a.dtype), kind="ExternalInput").ap())
    args.append(nc.dram_tensor("out_0", (1, S, D), F32, kind="ExternalOutput").ap())
    trunk(nc, *args)
    r = run_bass_kernel_spmd(nc, [arrays], core_ids=[0])
    return r.results[0]["out_0"]
```
